# Optimizing a Trainium2 kernel written in Bass

```python
import math
import jax
import jax.numpy as jnp
from jax import lax
import numpy as np

D_MODEL = 1024
BATCH = 1
SEQ = 1024
DEPTH = 1

CHUNK = 64

HEAD_DIM = 64
SB_HEADS = 8
SB_WIDTH = SB_HEADS * HEAD_DIM
SW_Q_HEADS = 8
SW_KV_HEADS = 2
SW_GROUP = SW_Q_HEADS // SW_KV_HEADS
SW_WIDTH = SW_Q_HEADS * HEAD_DIM
SW_KV_WIDTH = SW_KV_HEADS * HEAD_DIM
WINDOW = 128
WINDOW_CHUNKS = WINDOW // CHUNK
Q_BLOCK = 128
N_BRANCH = 2
IN_WIDTH = 3 * SB_WIDTH + SW_WIDTH + 2 * SW_KV_WIDTH + N_BRANCH * D_MODEL
IN_SPLITS = (SB_WIDTH, 2 * SB_WIDTH, 3 * SB_WIDTH,
             3 * SB_WIDTH + SW_WIDTH,
             3 * SB_WIDTH + SW_WIDTH + SW_KV_WIDTH,
             3 * SB_WIDTH + SW_WIDTH + 2 * SW_KV_WIDTH,
             3 * SB_WIDTH + SW_WIDTH + 2 * SW_KV_WIDTH + D_MODEL)

PEER_HEADS = 8
PEER_NKEYS = 128
PEER_EXPERTS = PEER_NKEYS * PEER_NKEYS
PEER_QDIM = 256
PEER_HALF = PEER_QDIM // 2
PEER_TOPK = 16
PEER_BLOCK = 128

RMS_EPS = 1e-6

kernel_name = 'hybrid_sb_swa_peer_adaln_block'

def _rmsnorm(x, g):
    xf = x.astype(jnp.float32)
    y = xf * lax.rsqrt(jnp.mean(xf * xf, axis=-1, keepdims=True) + RMS_EPS)
    return (y * g.astype(jnp.float32)).astype(x.dtype)

def _modulate(h, shift, scale):
    return h * (1.0 + scale[:, None, :]) + shift[:, None, :]

def _alibi_slopes(n_heads):
    return 2.0 ** (-8.0 * jnp.arange(1, n_heads + 1, dtype=jnp.float32) / n_heads)

def stick_breaking_attention(q, k, v):
    s_len = q.shape[2]
    scale = HEAD_DIM ** -0.5
    outs = []
    for qs in range(0, s_len, Q_BLOCK):
        ke = qs + Q_BLOCK
        z = jnp.einsum('bhqd,bhkd->bhqk', q[:, :, qs:ke], k[:, :, :ke]).astype(jnp.float32) * scale
        t_pos = qs + jnp.arange(Q_BLOCK, dtype=jnp.int32)[:, None]
        s_pos = jnp.arange(ke, dtype=jnp.int32)[None, :]
        mask = s_pos < t_pos
        log_keep = jnp.where(mask, -jax.nn.softplus(z), 0.0)
        suffix = lax.cumsum(log_keep, axis=3, reverse=True) - log_keep
        attn = jnp.where(mask, jnp.exp(jax.nn.log_sigmoid(z) + suffix), 0.0)
        outs.append(jnp.einsum('bhqk,bhkd->bhqd', attn.astype(v.dtype), v[:, :, :ke]))
    return jnp.concatenate(outs, axis=2)

def sliding_window_sink_attention(q, k, v, sinks):
    b, s_len, _ = q.shape
    n_chunks = s_len // CHUNK
    band = WINDOW_CHUNKS * CHUNK
    pad = WINDOW_CHUNKS - 1
    qc = q.reshape(b, n_chunks, CHUNK, SW_KV_HEADS, SW_GROUP, HEAD_DIM)
    kc = k.reshape(b, n_chunks, CHUNK, SW_KV_HEADS, HEAD_DIM)
    vc = v.reshape(b, n_chunks, CHUNK, SW_KV_HEADS, HEAD_DIM)
    pad_cfg = ((0, 0), (pad, 0), (0, 0), (0, 0), (0, 0))
    kp = jnp.pad(kc, pad_cfg)
    vp = jnp.pad(vc, pad_cfg)
    k_band = jnp.concatenate([kp[:, w:w + n_chunks] for w in range(WINDOW_CHUNKS)], axis=2)
    v_band = jnp.concatenate([vp[:, w:w + n_chunks] for w in range(WINDOW_CHUNKS)], axis=2)
    scores = jnp.einsum('bcqhgd,bckhd->bchgqk', qc, k_band).astype(jnp.float32) * (HEAD_DIM ** -0.5)
    q_off = jnp.arange(CHUNK, dtype=jnp.int32)
    k_off = jnp.arange(band, dtype=jnp.int32) - pad * CHUNK
    dist = jnp.abs(q_off[:, None] - k_off[None, :]).astype(jnp.float32)
    slopes = _alibi_slopes(SW_Q_HEADS).reshape(SW_KV_HEADS, SW_GROUP, 1, 1)
    scores = scores - slopes * dist
    k_abs = jnp.arange(n_chunks, dtype=jnp.int32)[:, None] * CHUNK + k_off[None, :]
    valid = (k_abs >= 0)[None, :, None, None, None, :]
    scores = jnp.where(valid, scores, -jnp.inf)
    sink = jnp.broadcast_to(sinks.astype(jnp.float32).reshape(SW_KV_HEADS, SW_GROUP, 1, 1),
                            scores.shape[:-1] + (1,))
    probs = jax.nn.softmax(jnp.concatenate([scores, sink], axis=-1), axis=-1)[..., :-1]
    out = jnp.einsum('bchgqk,bckhd->bcqhgd', probs.astype(v.dtype), v_band)
    return out.reshape(b, s_len, SW_WIDTH)

def peer_ffn(h, w_q, sub_keys, expert_u, expert_v):
    b, s_len, d = h.shape
    hb = h.reshape((b * s_len) // PEER_BLOCK, PEER_BLOCK, d)

    def block(xb):
        q = (xb @ w_q).reshape(PEER_BLOCK, PEER_HEADS, 2, PEER_HALF)
        sub_s = jnp.einsum('thpc,hpnc->thpn', q, sub_keys).astype(jnp.float32)
        top_s, top_i = lax.top_k(sub_s, PEER_TOPK)
        cand_s = top_s[:, :, 0, :, None] + top_s[:, :, 1, None, :]
        cand_i = top_i[:, :, 0, :, None] * PEER_NKEYS + top_i[:, :, 1, None, :]
        best_s, best_j = lax.top_k(cand_s.reshape(PEER_BLOCK, PEER_HEADS, PEER_TOPK * PEER_TOPK), PEER_TOPK)
        experts = jnp.take_along_axis(cand_i.reshape(PEER_BLOCK, PEER_HEADS, PEER_TOPK * PEER_TOPK),
                                      best_j, axis=-1)
        gate = jax.nn.softmax(best_s, axis=-1)
        act = jax.nn.gelu(jnp.einsum('td,thkd->thk', xb, expert_u[experts]), approximate=False)
        w = (gate * act.astype(jnp.float32)).astype(xb.dtype)
        return jnp.einsum('thk,thkd->td', w, expert_v[experts])

    return lax.map(block, hb).reshape(b, s_len, d)

def setup_inputs(seed: int = 0) -> dict:
    key = jax.random.key(seed)
    ks = jax.random.split(key, 16)
    f32 = jnp.float32
    d = D_MODEL
    return {
        'x': jax.random.normal(ks[0], (BATCH, SEQ, d), f32),
        'c': jax.random.normal(ks[1], (BATCH, d), f32),
        'w_ada': jax.random.normal(ks[2], (DEPTH, d, 6 * d), f32) * d ** -0.5,
        'b_ada': jax.random.normal(ks[3], (DEPTH, 6 * d), f32) * 0.01,
        'norm1_g': 1.0 + 0.02 * jax.random.normal(ks[4], (DEPTH, d), f32),
        'w_in': jax.random.normal(ks[5], (DEPTH, d, IN_WIDTH), f32) * d ** -0.5,
        'sb_proj': jax.random.normal(ks[6], (DEPTH, SB_WIDTH, d), f32) * SB_WIDTH ** -0.5,
        'sw_proj': jax.random.normal(ks[7], (DEPTH, SW_WIDTH, d), f32) * SW_WIDTH ** -0.5,
        'sw_sinks': jax.random.normal(ks[8], (DEPTH, SW_Q_HEADS), f32),
        'w_out': jax.random.normal(ks[9], (DEPTH, d, d), f32) * d ** -0.5,
        'norm2_g': 1.0 + 0.02 * jax.random.normal(ks[10], (DEPTH, d), f32),
        'peer_wq': jax.random.normal(ks[11], (DEPTH, d, PEER_HEADS * PEER_QDIM), f32) * d ** -0.5,
        'peer_sub_keys': jax.random.normal(ks[12], (DEPTH, PEER_HEADS, 2, PEER_NKEYS, PEER_HALF), f32) * PEER_HALF ** -0.5,
        'peer_u': jax.random.normal(ks[13], (DEPTH, PEER_EXPERTS, d), f32) * d ** -0.5,
        'peer_v': jax.random.normal(ks[14], (DEPTH, PEER_EXPERTS, d), f32) * PEER_HEADS ** -0.5,
        'final_g': 1.0 + 0.02 * jax.random.normal(ks[15], (d,), f32),
    }

def reference(x, c, w_ada, b_ada, norm1_g, w_in, sb_proj, sw_proj, sw_sinks, w_out,
              norm2_g, peer_wq, peer_sub_keys, peer_u, peer_v, final_g):
    b, s_len, _ = x.shape
    for l in range(DEPTH):
        mod = jax.nn.silu(c) @ w_ada[l] + b_ada[l]
        shift1, scale1, gate1, shift2, scale2, gate2 = jnp.split(mod, 6, axis=-1)

        h = _modulate(_rmsnorm(x, norm1_g[l]), shift1, scale1)
        proj = h @ w_in[l]
        qa, ka, va, qb, kb, vb, ga, gb = jnp.split(proj, IN_SPLITS, axis=-1)
        heads = lambda t: t.reshape(b, s_len, SB_HEADS, HEAD_DIM).transpose(0, 2, 1, 3)
        y_sb = stick_breaking_attention(heads(qa), heads(ka), heads(va))
        y_sb = y_sb.transpose(0, 2, 1, 3).reshape(b, s_len, SB_WIDTH)
        y_sw = sliding_window_sink_attention(qb, kb, vb, sw_sinks[l])
        merged = jax.nn.sigmoid(ga) * (y_sb @ sb_proj[l]) + jax.nn.sigmoid(gb) * (y_sw @ sw_proj[l])
        x = x + gate1[:, None, :] * (merged @ w_out[l])

        h2 = _modulate(_rmsnorm(x, norm2_g[l]), shift2, scale2)
        x = x + gate2[:, None, :] * peer_ffn(h2, peer_wq[l], peer_sub_keys[l], peer_u[l], peer_v[l])
    return _rmsnorm(x, final_g)


_drawn_inputs = setup_inputs


def setup_inputs(seed=0):
    import zlib

    import numpy as np

    out = dict(_drawn_inputs(seed))
    spreads = {}
    factors = {'b_ada': 3.125,
     'norm1_g': 3.929,
     'sw_sinks': 187.392,
     'norm2_g': 10.487,
     'final_g': 22.541}
    for name, (base, spread) in spreads.items():
        noise = np.random.default_rng([zlib.crc32(name.encode()), seed]).standard_normal(out[name].shape)
        drawn = base * np.exp(spread * noise) if base else spread * noise
        out[name] = jnp.asarray(drawn.astype(out[name].dtype))
    for name, factor in factors.items():
        out[name] = (out[name] * factor).astype(out[name].dtype)
    return out
```

```python
from contextlib import ExitStack

import numpy as np

import concourse.bass as bass
from concourse import mybir

F32 = mybir.dt.float32
U32 = mybir.dt.uint32
BF16 = mybir.dt.bfloat16
ALU = mybir.AluOpType
ACT = mybir.ActivationFunctionType
AX = mybir.AxisListType.X

P = 128
D = 1024
S = 1024
KT = D // P
NB = S // P
HALF = 512
DH = 64
SCALE = DH ** -0.5
SB_PAIRS = 4
SW_HEADS = 8
CHUNK = 64
BAND = 3 * CHUNK
HEADS = 8
NKEYS = 128
TOPK = 16
PICKS = NB * TOPK
RING = 8
EPS = 1e-6
LOWEST = -3.0e38
LED = 1

HT = 0
R4 = 8192
R2 = 16384
R3 = 24576
R1 = 32768
MODS = 40960
ARENA = MODS + 6 * D
SHIFT1, SCALE1, GATE1, SHIFT2, SCALE2, GATE2 = range(6)


class Chain:

    def __init__(self, eng, sem):
        self.eng, self.sem, self.n, self.turn, self.per = eng, sem, 0, None, 0

    def __call__(self, ins):
        ins.then_inc(self.sem, 1)
        self.n += 1
        more = 0 if self.turn is None else self.turn * self.per
        self.eng.wait_ge(self.sem, more + self.n)

    def enter(self, turn, per):
        self.turn, self.per, self.at = turn, per, self.n

    def leave(self, turns):
        assert self.n - self.at == self.per, (self.n - self.at, self.per)
        self.n = self.at + turns * self.per
        self.turn = None


def apart(eng, steps):
    eng.sem_inc(steps, 1)


def lead(eng, *semaphores):
    for s in semaphores:
        eng.sem_inc(s, LED)


def stick_chunks():
    out = []
    for e in range(2):
        for s in reversed(range(NB)):
            cuts = [(HALF, S), (s * P, HALF)] if s < 4 else [(s * P, S)]
            out += [(e, s, lo, hi) for lo, hi in cuts]
    return out


def build(nc, x, c8, w_ada, b_ada, g1, g2, gf, w_sb, w_sw, sinks, w_mg, w_out, w_q, sk, uv, consts, x1_dram, out):
    with ExitStack() as ctx:
        def sb(name, shape, dt=F32):
            return ctx.enter_context(nc.sbuf_tensor(name, shape, dt))

        def sem(name):
            return ctx.enter_context(nc.semaphore(name))

        arena = sb("arena", [P, ARENA])
        ident = sb("ident", [P, P])
        tri = sb("tri", [P, P])
        negones = sb("negones", [P, P])
        ident_b = sb("ident_b", [P, P], BF16)
        unseen_b = sb("unseen_b", [P, P], BF16)
        iota16 = sb("iota16", [P, TOPK])
        big = sb("big", [P, 2048])
        stats = sb("stats", [P, 32])
        sink_row = sb("sink_row", [P, SW_HEADS])
        small = sb("small", [P, 64])
        pb = ctx.enter_context(nc.psum_tensor("pb", [P, 8, HALF], F32))

        def at(off, n):
            return arena[:, off:off + n]

        def mod(v):
            return at(MODS + v * D, D)

        def rows(off, a, b):
            return at(off, a * b).rearrange("p (a b) -> p a b", a=a)

        hT = rows(HT, KT, S)

        dve_steps = sem("dve_steps")
        pool_steps = sem("pool_steps")
        in_small = sem("in_small")
        in_consts = sem("in_consts")
        in_rows = sem("in_rows")
        in_x = sem("in_x")
        in_ada = [sem(f"in_ada{i}") for i in range(4)]
        in_wsb = sem("in_wsb")
        in_wsw = sem("in_wsw")
        sig_c = sem("sig_c")
        c_wide = sem("c_wide")
        ada_mm = sem("ada_mm")
        ada_act = sem("ada_act")
        ada_dve = sem("ada_dve")
        sq_done = sem("sq_done")
        rinv = sem("rinv")
        rstd_done = sem("rstd_done")
        h_done = sem("h_done")
        tr_done = sem("tr_done")
        tr_act = sem("tr_act")
        tr_dve = sem("tr_dve")
        dve_own = sem("dve_own")
        wada = rows(R4, 4, 4096)
        cb = rows(R1, KT, P)
        brow = arena[0:1, R1 + 1024:R1 + 1024 + 6 * D]
        xt = rows(R3, NB, D)
        chain_at = [0]
        TABLE = SW_HEADS * BAND
        DVE_HALVES = (2, 3, 8, 9)

        def evacuations(j):
            mine = [i for i in range(12) if (i in DVE_HALVES) == (j in DVE_HALVES)]
            return (ada_dve if j in DVE_HALVES else ada_act), mine.index(j) + 1

        with nc.Block() as block:
            @block.sync
            def _(sp):
                sp.dma_start(small[:, 0:KT], c8).then_inc(in_small, 16)
                sp.dma_start(brow, b_ada).then_inc(in_rows, 16)
                for j in range(4):
                    sp.dma_start(wada[:, j, :], w_ada[j].rearrange("p k n -> p (k n)")).then_inc(in_ada[j % 4], 16)
                    if j == 1:
                        sp.dma_start(xt, x.rearrange("(b p) d -> p b d", p=P)).then_inc(in_x, 16)
                sp.dma_start(mod(SCALE1), g1.partition_broadcast(P)).then_inc(in_rows, 16)
                sp.dma_start(mod(SCALE2), g2.partition_broadcast(P)).then_inc(in_rows, 16)
                sp.dma_start(sink_row[:], sinks.partition_broadcast(P)).then_inc(in_rows, 16)
                for j in range(4, 12):
                    sp.wait_ge(ada_mm, j - 3)
                    sp.dma_start(wada[:, j % 4, :], w_ada[j].rearrange("p k n -> p (k n)")).then_inc(in_ada[j % 4], 16)
                sp.wait_ge(ada_mm, 12)
                sp.dma_start(at(R4, 3072), w_sb[0]).then_inc(in_wsb, 16)
                sp.dma_start(at(R2, 6144), w_sw).then_inc(in_wsw, 16)

            @block.gpsimd
            def _(pool):
                pool.dma_start(ident[:], consts[:, 0:P]).then_inc(in_consts, 16)
                pool.dma_start(tri[:], consts[:, P:2 * P]).then_inc(in_consts, 16)
                pool.dma_start(iota16[:], consts[:, 2 * P:2 * P + TOPK]).then_inc(in_consts, 16)
                pool.dma_start(big[:, 0:TABLE + P], consts[:, 2 * P + TOPK:2 * P + TOPK + TABLE + P]).then_inc(in_consts, 16)

            @block.scalar
            def _(act):
                act.wait_ge(in_small, 16)
                act.activation(small[:, 8:16], small[:, 0:8], ACT.Sigmoid).then_inc(sig_c, 1)
                act.wait_ge(in_x, 16)
                for b in range(NB):
                    act.wait_ge(sq_done, b)
                    act.activation(pb[:, 4:6, :].rearrange("p a b -> p (a b)"), xt[:, b, :], ACT.Square,
                                   accum_out=stats[:, b:b + 1]).then_inc(sq_done, 1)
                for j in (0, 1):
                    act.wait_ge(ada_mm, j + 1)
                    act.activation(mod(SHIFT1)[:, j * HALF:(j + 1) * HALF], pb[:, j % 4, :], ACT.Copy).then_inc(ada_act, 1)
                act.wait_ge(rinv, 1)
                act.activation(stats[:, 16:24], stats[:, 8:16], ACT.Sqrt).then_inc(rstd_done, 1)
                for b in range(NB):
                    act.wait_ge(tr_done, 2 * b + 1)
                    act.activation(hT[:, 0:4, b * P:(b + 1) * P], pb[:, 4 + 2 * (b % 2), :].rearrange("p (a b) -> p a b", a=4),
                                   ACT.Copy).then_inc(tr_act, 1)
                    j = 4 + b
                    if j not in DVE_HALVES:
                        act.wait_ge(ada_mm, j + 1)
                        act.activation(mod(j // 2)[:, (j % 2) * HALF:(j % 2 + 1) * HALF], pb[:, j % 4, :],
                                       ACT.Copy).then_inc(ada_act, 1)

            @block.vector
            def _(dve):
                link = Chain(dve, dve_own)

                def scale_half(j):
                    dve.wait_ge(ada_mm, j + 1)
                    row = mod(j // 2)[:, (j % 2) * HALF:(j % 2 + 1) * HALF]
                    dve.scalar_tensor_tensor(out=row, in0=pb[:, j % 4, :], scalar=1.0, in1=row, op0=ALU.add,
                                             op1=ALU.mult).then_inc(ada_dve, 1)

                dve.memset(negones[:], -1.0)
                dve.wait_ge(in_consts, 64)
                dve.tensor_copy(ident_b[:], ident[:])
                dve.tensor_copy(unseen_b[:], big[:, TABLE:TABLE + P])
                link(dve.memset(small[:, 32:33], 1.0))
                dve.wait_ge(sig_c, 1)
                link(dve.tensor_tensor(small[:, 16:24], small[:, 0:8], small[:, 8:16], ALU.mult))
                dve.tensor_copy(cb, small[:, 16:24].unsqueeze(2).to_broadcast([P, KT, P])).then_inc(c_wide, 1)
                dve.wait_ge(sq_done, NB)
                link(dve.tensor_scalar(stats[:, 24:32], stats[:, 0:8], 1.0 / D, EPS, ALU.mult, ALU.add))
                dve.reciprocal(stats[:, 8:16], stats[:, 24:32]).then_inc(rinv, 1)
                dve.wait_ge(in_rows, 64)
                scale_half(2)
                scale_half(3)
                dve.wait_ge(ada_dve, 2)
                dve.wait_ge(ada_act, 2)
                dve.wait_ge(rstd_done, 1)
                for b in range(NB):
                    link(dve.scalar_tensor_tensor(out=xt[:, b, :], in0=xt[:, b, :], scalar=stats[:, 16 + b:17 + b],
                                                  in1=mod(SCALE1), op0=ALU.mult, op1=ALU.mult))
                    dve.tensor_tensor(xt[:, b, :], xt[:, b, :], mod(SHIFT1), ALU.add).then_inc(h_done, 1)
                    if b:
                        a = b - 1
                        dve.wait_ge(tr_done, 2 * a + 2)
                        dve.tensor_copy(hT[:, 4:8, a * P:(a + 1) * P],
                                        pb[:, 5 + 2 * (a % 2), :].rearrange("p (a b) -> p a b", a=4)).then_inc(tr_dve, 1)
                    if b and 3 + b in DVE_HALVES:
                        scale_half(3 + b)
                a = NB - 1
                dve.wait_ge(tr_done, 2 * a + 2)
                dve.tensor_copy(hT[:, 4:8, a * P:(a + 1) * P],
                                pb[:, 5 + 2 * (a % 2), :].rearrange("p (a b) -> p a b", a=4)).then_inc(tr_dve, 1)
                chain_at[0] = link.n

            @block.tensor
            def _(pe):
                def modulation_half(j):
                    pe.wait_ge(in_ada[j % 4], 16 * (j // 4 + 1))
                    if j >= 4:
                        pe.wait_ge(*evacuations(j - 4))
                    w = wada[:, j % 4, :].rearrange("p (k n) -> p k n", k=KT)
                    for k in range(KT):
                        pe.matmul(pb[:, j % 4, :], cb[:, k, :], w[:, k, :], start=(k == 0), stop=False)
                    pe.matmul(pb[:, j % 4, :], small[0:1, 32:33].to_broadcast([1, P]), brow[:, j * HALF:(j + 1) * HALF],
                              start=False, stop=True).then_inc(ada_mm, 1)

                pe.wait_ge(in_consts, 64)
                pe.wait_ge(c_wide, 1)
                pe.wait_ge(in_rows, 64)
                for j in range(4):
                    modulation_half(j)
                for b in range(NB):
                    pe.wait_ge(h_done, b + 1)
                    if b < 2:
                        pe.wait_ge(sq_done, NB)
                    else:
                        pe.wait_ge(tr_act, b - 1)
                        pe.wait_ge(tr_dve, b - 1)
                    for k in range(KT):
                        t = pe.transpose(pb[:, 4 + 2 * (b % 2) + k // 4, (k % 4) * P:(k % 4 + 1) * P],
                                         xt[:, b, k * P:(k + 1) * P], ident[:])
                        if k % 4 == 3:
                            t.then_inc(tr_done, 1)
                    modulation_half(4 + b)

        chunks = stick_chunks()
        NC = len(chunks)
        proj = sem("proj")
        proj_act = sem("proj_act")
        proj_dve = sem("proj_dve")
        z_done = sem("z_done")
        abs_done = sem("abs_done")
        e1_done = sem("e1_done")
        ln_done = sem("ln_done")
        sp_done = sem("sp_done")
        sums_done = sem("sums_done")
        att_done = sem("att_done")
        later_done = sem("later_done")
        pv_done = sem("pv_done")
        y_taken = sem("y_taken")
        dve_sb = sem("dve_sb")
        wsb = at(R4, 3072).rearrange("p (a k f) -> p a k f", a=3, k=KT)
        later = rows(R4 + 3072, 2, S)
        qT, kT = at(R1, S), at(R1 + S, S)
        v = rows(R1 + 2 * S, NB, P)
        zabs = rows(R1 + 3072, 3, HALF)
        spl = rows(R1 + 4608, 3, HALF)
        attn = rows(R1 + 6144, 3, HALF)
        ysbT = rows(R3, SB_PAIRS, S)
        yswT = rows(R3 + 4096, SB_PAIRS, S)

        with nc.Block() as block:
            @block.sync
            def _(sp):
                with sp.Fori(0, SB_PAIRS - 1) as t:
                    sp.wait_ge(proj, t * 6 + 6)
                    sp.dma_start(at(R4, 3072), w_sb[bass.ds(t + 1, 1)].rearrange("a p f -> (a p) f")).then_inc(in_wsb, 16)

            @block.scalar
            def _(act):
                lead(act, att_done, y_taken)
                with act.Fori(0, SB_PAIRS) as t:
                    for i, dst in enumerate((qT, qT, kT, kT)):
                        act.wait_ge(proj, t * 6 + i + 1)
                        act.activation(dst[:, (i % 2) * HALF:(i % 2 + 1) * HALF], pb[:, i, :], ACT.Copy,
                                       scale=SCALE if i < 2 else 1.0).then_inc(proj_act, 1)

                    def softplus_log(c):
                        n = chunks[c][3] - chunks[c][2]
                        a = zabs[:, c % 3, 0:n]
                        act.wait_ge(z_done, t * NC + c + 1)
                        act.wait_ge(sp_done, LED + t * NC + max(c - 2, 0))
                        act.activation(a, pb[:, c % 4, 0:n], ACT.Abs).then_inc(abs_done, 1)
                        act.wait_ge(abs_done, t * NC + c + 1)
                        act.activation(a, a, ACT.Exp, scale=-1.0).then_inc(e1_done, 1)
                        act.wait_ge(e1_done, t * NC + c + 1)
                        act.activation(a, a, ACT.Ln, bias=1.0).then_inc(ln_done, 1)

                    softplus_log(0)
                    softplus_log(1)
                    for c, (e, s, lo, hi) in enumerate(chunks):
                        act.wait_ge(sums_done, LED + t * NC + c + 1)
                        act.wait_ge(pv_done, LED + t * NC + max(c - 2, 0))
                        act.activation(attn[:, c % 3, 0:hi - lo], pb[:, c % 4, 0:hi - lo], ACT.Exp).then_inc(att_done, 1)
                        if c + 2 < NC:
                            softplus_log(c + 2)
                    act.wait_ge(pv_done, LED + t * NC + NC)
                    for i in range(2):
                        act.activation(ysbT[:, bass.ds(t, 1), i * HALF:(i + 1) * HALF].rearrange("p a b -> p (a b)"),
                                       pb[:, 6 + i, :], ACT.Copy).then_inc(y_taken, 1)

            @block.vector
            def _(dve):
                lead(dve, proj_dve, sp_done, later_done)
                with dve.Fori(0, SB_PAIRS) as t:
                    for i in range(2):
                        dve.wait_ge(proj, t * 6 + 5 + i)
                        dve.tensor_copy(v[:, 4 * i:4 * i + 4, :].rearrange("p a b -> p (a b)"), pb[:, 4 + i, :]).then_inc(proj_dve, 1)

                    for c, (e, s, lo, hi) in enumerate(chunks):
                        n = hi - lo
                        dve.wait_ge(ln_done, t * NC + c + 1)
                        dve.wait_ge(sums_done, LED + t * NC + max(c - 2, 0))
                        dve.scalar_tensor_tensor(out=spl[:, c % 3, 0:n], in0=pb[:, c % 4, 0:n], scalar=0.0,
                                                 in1=zabs[:, c % 3, 0:n], op0=ALU.max, op1=ALU.add).then_inc(sp_done, 1)
                        first = [i for i, k in enumerate(chunks) if k[:2] == (e, s)][0]
                        dve.wait_ge(sums_done, LED + t * NC + first)
                        dve.wait_ge(sp_done, LED + t * NC + c + 1)
                        dve.wait_ge(later_done, LED + t * NC + c)
                        own = lo == s * P
                        if own:
                            op = dve.tensor_copy(later[:, s % 2, lo:lo + P], spl[:, c % 3, 0:P])
                        a = lo + P if own else lo
                        if a < hi:
                            op = dve.tensor_tensor(later[:, s % 2, a:hi], later[:, (s + 1) % 2, a:hi],
                                                   spl[:, c % 3, a - lo:n], ALU.add)
                        op.then_inc(later_done, 1)

            @block.tensor
            def _(pe):
                lead(pe, sums_done, pv_done)
                with pe.Fori(0, SB_PAIRS) as t:
                    pe.wait_ge(in_wsb, t * 16 + 16)
                    pe.wait_ge(att_done, LED + t * NC)
                    for i in range(4):
                        for k in range(KT):
                            m = pe.matmul(pb[:, i, :], wsb[:, i // 2, k, :], hT[:, k, (i % 2) * HALF:(i % 2 + 1) * HALF],
                                          start=(k == 0), stop=(k == KT - 1))
                        m.then_inc(proj, 1)
                    pe.wait_ge(proj_dve, LED + t * 2)
                    for b in range(NB):
                        for k in range(KT):
                            m = pe.matmul(pb[:, 4 + b // 4, (b % 4) * P:(b % 4 + 1) * P], hT[:, k, b * P:(b + 1) * P],
                                          wsb[:, 2, k, :], start=(k == 0), stop=(k == KT - 1))
                        if b % 4 == 3:
                            m.then_inc(proj, 1)

                    def scores(c):
                        e, s, lo, hi = chunks[c]
                        pe.wait_ge(att_done, LED + t * NC + max(c - 3, 0))
                        m = pe.matmul(pb[:, c % 4, 0:hi - lo], kT[64 * e:64 * e + 64, s * P:(s + 1) * P],
                                      qT[64 * e:64 * e + 64, lo:hi], start=True, stop=True)
                        if lo == s * P:
                            m = pe.matmul(pb[:, c % 4, 0:P], ident_b[:], unseen_b[:], start=False, stop=True,
                                          skip_group_check=True)
                        m.then_inc(z_done, 1)

                    def values(c):
                        e, s, lo, hi = chunks[c]
                        pe.wait_ge(att_done, LED + t * NC + c + 1)
                        bank = 6 + lo // HALF
                        pe.matmul(pb[64 * e:64 * e + 64, bank, lo % HALF:lo % HALF + hi - lo], v[:, s, 64 * e:64 * e + 64],
                                  attn[:, c % 3, 0:hi - lo], start=s == (7 if lo >= HALF else 3), stop=s == 0,
                                  skip_group_check=True).then_inc(pv_done, 1)

                    pe.wait_ge(proj_act, t * 4 + 4)
                    pe.wait_ge(proj_dve, LED + t * 2 + 2)
                    for c in range(3):
                        scores(c)
                    for c, (e, s, lo, hi) in enumerate(chunks):
                        a = max(lo, (s + 1) * P)
                        pe.wait_ge(sp_done, LED + t * NC + c + 1)
                        m = pe.matmul(pb[:, c % 4, 0:hi - lo], tri[:], spl[:, c % 3, 0:hi - lo], start=False,
                                      stop=True, skip_group_check=True)
                        if a < hi:
                            behind = max(i for i, k in enumerate(chunks) if k[:2] == (e, s + 1) and k[2] < hi and k[3] > a)
                            pe.wait_ge(later_done, LED + t * NC + behind + 1)
                            m = pe.matmul(pb[:, c % 4, a - lo:hi - lo], negones[:], later[:, (s + 1) % 2, a:hi],
                                          start=False, stop=True, skip_group_check=True)
                        m.then_inc(sums_done, 1)
                        if c + 3 < NC:
                            scores(c + 3)
                        if c == 0:
                            pe.wait_ge(y_taken, LED + t * 2)
                        else:
                            values(c - 1)
                    values(NC - 1)

        sw_proj_done = sem("sw_proj_done")
        sw_act = sem("sw_act")
        sw_dve = sem("sw_dve")
        sc_done = sem("sc_done")
        biased = sem("biased")
        shifted = sem("shifted")
        exp_done = sem("exp_done")
        probs_done = sem("probs_done")
        pt_done = sem("pt_done")
        pt_act = sem("pt_act")
        pt_dve = sem("pt_dve")
        ysw_done = sem("ysw_done")
        ysw_taken = sem("ysw_taken")
        dve_sw = sem("dve_sw")
        in_wq = sem("in_wq")
        wsw = rows(R2, 6 * KT, P).rearrange("p (a k) f -> p a k f", a=6)
        qb = rows(R1, 4, S)
        kb = at(R1 + 4096, S)
        vb = rows(R1 + 5120, NB, P)
        prob = at(R1 + 6144, 2048).rearrange("p (h n) -> p h n", h=SW_HEADS)
        sc2 = rows(R4, 2, SW_HEADS * BAND)
        pT = at(R4 + 3072, 2048).rearrange("p (h w t) -> p h w t", h=SW_HEADS, w=2)
        peak = rows(R4 + 5120, 2, 8)
        sink_e = rows(R4 + 5136, 2, 8)
        total = rows(R4 + 5152, 2, 8)
        in_wmg = sem("in_wmg")

        with nc.Block() as block:
            @block.sync
            def _(sp):
                sp.dma_start(at(MODS, 2048), w_q[0]).then_inc(in_wq, 16)

            @block.tensor
            def _(pe):
                pe.wait_ge(in_wsw, 16)
                for j in range(4):
                    for i in range(2):
                        for k in range(KT):
                            m = pe.matmul(pb[:, 2 * j + i, :], wsw[:, j, k, :], hT[:, k, i * HALF:(i + 1) * HALF],
                                          start=(k == 0), stop=(k == KT - 1))
                        m.then_inc(sw_proj_done, 1)
                for i in range(2):
                    pe.wait_ge(sw_act if i == 0 else sw_dve, 1)
                    for k in range(KT):
                        m = pe.matmul(pb[:, i, :], wsw[:, 4, k, :], hT[:, k, i * HALF:(i + 1) * HALF],
                                      start=(k == 0), stop=(k == KT - 1))
                    m.then_inc(sw_proj_done, 1)
                for b in range(NB):
                    if b % 4 == 0:
                        pe.wait_ge(sw_act if b == 0 else sw_dve, 2)
                    for k in range(KT):
                        m = pe.matmul(pb[:, 2 + b // 4, (b % 4) * P:(b % 4 + 1) * P], hT[:, k, b * P:(b + 1) * P],
                                      wsw[:, 5, k, :], start=(k == 0), stop=(k == KT - 1))
                    if b % 4 == 3:
                        m.then_inc(sw_proj_done, 1)
                pe.wait_ge(sw_act, 6)
                pe.wait_ge(sw_dve, 6)

                def scores(b):
                    off = CHUNK if b == 0 else 0
                    if b:
                        pe.wait_ge(biased, b)
                    for g in range(2):
                        for j in range(4):
                            a = (j % 2) * BAND
                            m = pe.matmul(pb[:, 2 * g + j // 2, a + off:a + BAND], qb[64 * g:64 * g + 64, j, b * P:(b + 1) * P],
                                          kb[64 * g:64 * g + 64, b * P - CHUNK + off:(b + 1) * P], start=True, stop=True)
                    m.then_inc(sc_done, 1)

                scores(0)
                for b in range(NB):
                    if b + 1 < NB:
                        scores(b + 1)
                    pe.wait_ge(probs_done, b + 1)
                    for r in range(2):
                        if b and r == 0:
                            pe.wait_ge(pt_act, 2 * b)
                            pe.wait_ge(ysw_taken, b)
                        if b and r == 1:
                            pe.wait_ge(pt_dve, 2 * b)
                        for h in range(4 * r, 4 * r + 4):
                            for w in range(1 if b == 0 else 0, 2):
                                q = (h % 4) * 2 + w
                                m = pe.transpose(pb[:, 4 + 2 * r + q // 4, (q % 4) * P:(q % 4 + 1) * P],
                                                 prob[:, h, w * P:(w + 1) * P], ident[:])
                        m.then_inc(pt_done, 1)
                    pe.wait_ge(pt_act, 2 * b + 2)
                    pe.wait_ge(pt_dve, 2 * b + 2)
                    for h in range(SW_HEADS):
                        g, j = h // 4, h % 4
                        for w in range(1 if b == 0 else 0, 2):
                            m = pe.matmul(pb[64 * g:64 * g + 64, 4, j * P:(j + 1) * P], vb[:, b - 1 + w, 64 * g:64 * g + 64],
                                          pT[:, h, w, :], start=(w == 0 or b == 0), stop=(w == 1))
                    m.then_inc(ysw_done, 1)

            @block.scalar
            def _(act):
                for j in range(4):
                    act.wait_ge(sw_proj_done, 2 * j + 1)
                    act.activation(qb[:, j, 0:HALF], pb[:, 2 * j, :], ACT.Copy).then_inc(sw_act, 1)
                act.wait_ge(sw_proj_done, 9)
                act.activation(kb[:, 0:HALF], pb[:, 0, :], ACT.Copy).then_inc(sw_act, 1)
                act.wait_ge(sw_proj_done, 11)
                act.activation(vb[:, 0:4, :].rearrange("p a b -> p (a b)"), pb[:, 2, :], ACT.Copy).then_inc(sw_act, 1)

                def exponentials(b):
                    act.wait_ge(shifted, b + 1)
                    act.activation(sink_e[:, b % 2, :], sink_e[:, b % 2, :], ACT.Exp)
                    s = sc2[:, b % 2, :].rearrange("p (h n) -> p h n", h=SW_HEADS)[:, :, (CHUNK if b == 0 else 0):]
                    act.activation(s, s, ACT.Exp).then_inc(exp_done, 1)

                exponentials(0)
                for b in range(NB):
                    if b + 1 < NB:
                        exponentials(b + 1)
                    w0 = 1 if b == 0 else 0
                    act.wait_ge(pt_done, 2 * b + 1)
                    if b:
                        act.wait_ge(ysw_done, b)
                    for i in range(2):
                        act.activation(pT[:, 2 * i:2 * i + 2, w0:, :], pb[:, 4 + i, :].rearrange("p (h w t) -> p h w t", h=2, w=2)[:, :, w0:, :],
                                       ACT.Copy).then_inc(pt_act, 1)
                    act.wait_ge(ysw_done, b + 1)
                    act.activation(yswT[:, :, b * P:(b + 1) * P], pb[:, 4, :].rearrange("p (j t) -> p j t", j=4),
                                   ACT.Copy).then_inc(ysw_taken, 1)

            @block.vector
            def _(dve):
                link = Chain(dve, dve_sw)
                link(dve.memset(prob[:, :, 0:CHUNK], 0.0))
                for j in range(4):
                    dve.wait_ge(sw_proj_done, 2 * j + 2)
                    dve.tensor_copy(qb[:, j, HALF:S], pb[:, 2 * j + 1, :]).then_inc(sw_dve, 1)
                dve.wait_ge(sw_proj_done, 10)
                dve.tensor_copy(kb[:, HALF:S], pb[:, 1, :]).then_inc(sw_dve, 1)
                dve.wait_ge(sw_proj_done, 12)
                dve.tensor_copy(vb[:, 4:8, :].rearrange("p a b -> p (a b)"), pb[:, 3, :]).then_inc(sw_dve, 1)

                def part(b):
                    off = CHUNK if b == 0 else 0
                    return sc2[:, b % 2, :].rearrange("p (h n) -> p h n", h=SW_HEADS)[:, :, off:], BAND - off

                def shift(b):
                    s, n = part(b)
                    dve.wait_ge(sc_done, b + 1)
                    if b == 0:
                        for q in range(4):
                            k = slice(2 * q, 2 * q + 2)
                            t = big[:, 0:TABLE].rearrange("p (h n) -> p h n", h=SW_HEADS)
                            op = dve.scalar_tensor_tensor(out=s[:, k, :], in0=pb[:, q, 0:2 * BAND].rearrange("p (h n) -> p h n", h=2)[:, :, CHUNK:],
                                                          scalar=SCALE, in1=t[:, k, CHUNK:], op0=ALU.mult, op1=ALU.add)
                    else:
                        op = dve.scalar_tensor_tensor(out=sc2[:, b % 2, :].rearrange("p (q n) -> p q n", q=4), in0=pb[:, 0:4, 0:2 * BAND],
                                                      scalar=SCALE, in1=big[:, 0:TABLE].rearrange("p (q n) -> p q n", q=4),
                                                      op0=ALU.mult, op1=ALU.add)
                    op.then_inc(biased, 1)
                    dve.wait_ge(biased, b + 1)
                    link(dve.tensor_reduce(peak[:, b % 2, :], s, AX, ALU.max))
                    link(dve.tensor_tensor(peak[:, b % 2, :], peak[:, b % 2, :], sink_row[:], ALU.max))
                    link(dve.tensor_tensor(sink_e[:, b % 2, :], sink_row[:], peak[:, b % 2, :], ALU.subtract))
                    dve.tensor_tensor(s, s, peak[:, b % 2, :].unsqueeze(2).to_broadcast([P, SW_HEADS, n]),
                                      ALU.subtract).then_inc(shifted, 1)

                shift(0)
                for b in range(NB):
                    if b + 1 < NB:
                        shift(b + 1)
                    s, n = part(b)
                    dve.wait_ge(exp_done, b + 1)
                    link(dve.tensor_reduce(total[:, b % 2, :], s, AX, ALU.add))
                    link(dve.tensor_tensor(total[:, b % 2, :], total[:, b % 2, :], sink_e[:, b % 2, :], ALU.add))
                    link(dve.reciprocal(total[:, b % 2, :], total[:, b % 2, :]))
                    if b:
                        dve.wait_ge(pt_done, 2 * b)
                    dve.tensor_tensor(prob[:, :, 256 - n:], s, total[:, b % 2, :].unsqueeze(2).to_broadcast([P, SW_HEADS, n]),
                                      ALU.mult).then_inc(probs_done, 1)
                    w0 = 1 if b == 0 else 0
                    dve.wait_ge(pt_done, 2 * b + 2)
                    if b:
                        dve.wait_ge(ysw_done, b)
                    for i in range(2):
                        dve.tensor_copy(pT[:, 4 + 2 * i:6 + 2 * i, w0:, :], pb[:, 6 + i, :].rearrange("p (h w t) -> p h w t", h=2, w=2)[:, :, w0:, :]).then_inc(pt_dve, 1)

        gate_mm = sem("gate_mm")
        gate_sig = sem("gate_sig")
        branch_mm = sem("branch_mm")
        gated = sem("gated")
        merged_done = sem("merged_done")
        in_wout = sem("in_wout")
        in_wmg2 = [sem("in_wmg0"), sem("in_wmg1")]
        wmg = at(R4, 6144).rearrange("p (u k f) -> p u k f", u=2, k=24)
        sig = rows(R4 + 6144, 4, HALF)
        mergedT = rows(R2, KT, S)
        wout = rows(R1, KT, D)

        with nc.Block() as block:
            @block.sync
            def _(sp):
                for u in range(2):
                    sp.dma_start(at(R4 + 3072 * u, 3072), w_mg[u]).then_inc(in_wmg2[u], 16)
                sp.dma_start(at(R1, 8192), w_out).then_inc(in_wout, 16)
                with sp.Fori(0, KT // 2 - 1) as t:
                    for u in range(2):
                        sp.wait_ge(branch_mm, t * 8 + 4 * u + 4)
                        sp.dma_start(at(R4 + 3072 * u, 3072), w_mg[bass.ds(t * 2 + 2 + u, 1)].rearrange("a p f -> (a p) f")).then_inc(in_wmg2[u], 16)

            @block.tensor
            def _(pe):
                with pe.Fori(0, KT // 2) as t:
                    for u in range(2):
                        pe.wait_ge(in_wmg2[u], t * 16 + 16)
                        for q in range(4):
                            pe.wait_ge(gate_sig, LED + t * 8 + 4 * u)
                            for k in range(KT):
                                m = pe.matmul(pb[:, q, :], wmg[:, u, (q // 2) * KT + k, :], hT[:, k, (q % 2) * HALF:(q % 2 + 1) * HALF],
                                              start=(k == 0), stop=(k == KT - 1))
                            m.then_inc(gate_mm, 1)
                        pe.wait_ge(gated, LED + t * 8 + 4 * u)
                        for q in range(4):
                            y = ysbT if q < 2 else yswT
                            for k in range(4):
                                m = pe.matmul(pb[:, 4 + q, :], wmg[:, u, 16 + (q // 2) * 4 + k, :], y[:, k, (q % 2) * HALF:(q % 2 + 1) * HALF],
                                              start=(k == 0), stop=(k == 3))
                            m.then_inc(branch_mm, 1)

            @block.scalar
            def _(act):
                lead(act, gate_sig)
                with act.Fori(0, KT // 2) as t:
                    for u in range(2):
                        act.wait_ge(merged_done, LED + t * 4 + 2 * u)
                        for q in range(4):
                            act.wait_ge(gate_mm, t * 8 + 4 * u + q + 1)
                            act.activation(sig[:, q, :], pb[:, q, :], ACT.Sigmoid).then_inc(gate_sig, 1)

            @block.vector
            def _(dve):
                lead(dve, gated, merged_done)
                with dve.Fori(0, KT // 2) as t:
                    for u in range(2):
                        for q in range(4):
                            dve.wait_ge(gate_sig, LED + t * 8 + 4 * u + q + 1)
                            dve.wait_ge(branch_mm, t * 8 + 4 * u + q + 1)
                            dve.tensor_tensor(sig[:, q, :], sig[:, q, :], pb[:, 4 + q, :], ALU.mult).then_inc(gated, 1)
                        dve.wait_ge(gated, LED + t * 8 + 4 * u + 4)
                        for i in range(2):
                            dve.tensor_tensor(mergedT[:, bass.ds(t * 2 + u, 1), i * HALF:(i + 1) * HALF].rearrange("p a b -> p (a b)"),
                                              sig[:, i, :], sig[:, 2 + i, :], ALU.add).then_inc(merged_done, 1)

        out_mm = sem("out_mm")
        x1_scaled = sem("x1_scaled")
        x1_done = sem("x1_done")
        x1_square = sem("x1_square")
        in_x2 = sem("in_x2")
        rinv2 = sem("rinv2")
        rstd2 = sem("rstd2")
        h2_done = sem("h2_done")
        tr2_done = sem("tr2_done")
        tr2_act = sem("tr2_act")
        tr2_dve = sem("tr2_dve")
        dve_o = sem("dve_o")
        x1_stored = sem("x1_stored")
        h2 = rows(R4, NB, D)
        h2T = hT

        with nc.Block() as block:
            @block.sync
            def _(sp):
                sp.dma_start(xt, x.rearrange("(b p) d -> p b d", p=P)).then_inc(in_x2, 16)
                for b in range(NB):
                    sp.wait_ge(x1_done, b + 1)
                    sp.dma_start(x1_dram[b * P:(b + 1) * P, :], xt[:, b, :]).then_inc(x1_stored, 16)

            @block.tensor
            def _(pe):
                def transposes(b):
                    pe.wait_ge(h2_done, b + 1)
                    if b >= 2:
                        pe.wait_ge(tr2_act, b - 1)
                        pe.wait_ge(tr2_dve, b - 1)
                    for k in range(KT):
                        t = pe.transpose(pb[:, 4 + 2 * (b % 2) + k // 4, (k % 4) * P:(k % 4 + 1) * P],
                                         h2[:, b, k * P:(k + 1) * P], ident[:])
                        if k % 4 == 3:
                            t.then_inc(tr2_done, 1)

                pe.wait_ge(in_wout, 16)
                for b in range(NB):
                    if b >= 2:
                        pe.wait_ge(x1_scaled, b - 1)
                    for i in range(2):
                        for k in range(KT):
                            m = pe.matmul(pb[:, 2 * (b % 2) + i, :], mergedT[:, k, b * P:(b + 1) * P], wout[:, k, i * HALF:(i + 1) * HALF],
                                          start=(k == 0), stop=(k == KT - 1))
                    m.then_inc(out_mm, 1)
                    if b:
                        transposes(b - 1)
                transposes(NB - 1)

            @block.scalar
            def _(act):
                for b in range(NB):
                    act.wait_ge(x1_done, b + 1)
                    act.activation(h2[:, b, :], xt[:, b, :], ACT.Square, accum_out=stats[:, b:b + 1]).then_inc(x1_square, 1)
                    act.wait_ge(rinv2, b + 1)
                    act.activation(stats[:, 16 + b:17 + b], stats[:, 8 + b:9 + b], ACT.Sqrt).then_inc(rstd2, 1)
                    if b:
                        act.wait_ge(tr2_done, 2 * b - 1)
                        act.activation(h2T[:, 0:4, (b - 1) * P:b * P], pb[:, 4 + 2 * ((b - 1) % 2), :].rearrange("p (a b) -> p a b", a=4),
                                       ACT.Copy).then_inc(tr2_act, 1)
                act.wait_ge(tr2_done, 2 * NB - 1)
                act.activation(h2T[:, 0:4, S - P:S], pb[:, 4 + 2 * ((NB - 1) % 2), :].rearrange("p (a b) -> p a b", a=4),
                               ACT.Copy).then_inc(tr2_act, 1)

            @block.vector
            def _(dve):
                link = Chain(dve, dve_o)

                def residual(b):
                    dve.wait_ge(out_mm, b + 1)
                    dve.tensor_tensor(h2[:, b, :], pb[:, 2 * (b % 2):2 * (b % 2) + 2, :].rearrange("p a b -> p (a b)"), mod(GATE1),
                                      ALU.mult).then_inc(x1_scaled, 1)
                    dve.wait_ge(x1_scaled, b + 1)
                    dve.tensor_tensor(xt[:, b, :], xt[:, b, :], h2[:, b, :], ALU.add).then_inc(x1_done, 1)

                def take(b):
                    dve.wait_ge(tr2_done, 2 * b + 2)
                    dve.tensor_copy(h2T[:, 4:8, b * P:(b + 1) * P],
                                    pb[:, 5 + 2 * (b % 2), :].rearrange("p (a b) -> p a b", a=4)).then_inc(tr2_dve, 1)

                dve.wait_ge(in_x2, 16)
                residual(0)
                for b in range(NB):
                    if b + 1 < NB:
                        residual(b + 1)
                    dve.wait_ge(x1_square, b + 1)
                    link(dve.tensor_scalar(stats[:, 24 + b:25 + b], stats[:, b:b + 1], 1.0 / D, EPS, ALU.mult, ALU.add))
                    dve.reciprocal(stats[:, 8 + b:9 + b], stats[:, 24 + b:25 + b]).then_inc(rinv2, 1)
                    if b:
                        take(b - 1)
                    dve.wait_ge(rstd2, b + 1)
                    link(dve.scalar_tensor_tensor(out=h2[:, b, :], in0=xt[:, b, :], scalar=stats[:, 16 + b:17 + b],
                                                  in1=mod(SCALE2), op0=ALU.mult, op1=ALU.mult))
                    dve.tensor_tensor(h2[:, b, :], h2[:, b, :], mod(SHIFT2), ALU.add).then_inc(h2_done, 1)
                take(NB - 1)

        gathered = [sem(f"gathered{i}") for i in range(RING)]
        ring_free = sem("ring_free")
        acc_free = sem("acc_free")
        zeroed = sem("zeroed")
        in_wqn = sem("in_wqn")
        q_mm = sem("q_mm")
        q_taken = sem("q_taken")
        s_mm = sem("s_mm")
        s_taken = sem("s_taken")
        s_used = sem("s_used")
        picked = sem("picked")
        picked_exp = sem("picked_exp")
        published = sem("published")
        dots_done = sem("dots_done")
        gelu_done = sem("gelu_done")
        diag_done = sem("diag_done")
        idg_done = sem("idg_done")
        dve_p = sem("dve_p")
        ring = rows(R3, RING, 2 * D)
        acc = rows(R2, NB, D)
        wq = at(MODS, 2048).rearrange("p (a k f) -> p a k f", a=2, k=KT)
        qpT = at(MODS + 2 * D, S)
        ssb = rows(MODS + 3 * D, NB, NKEYS)
        tiny = MODS + 4 * D
        vals = [rows(tiny + 128 * i, NB, TOPK) for i in range(2)]
        best = rows(tiny + 256, NB, TOPK)
        fl = [rows(tiny + 384 + 128 * i, NB, TOPK) for i in range(2)]
        res = [rows(tiny + 640 + 128 * i, NB, TOPK) for i in range(2)]
        gate_next = rows(tiny + 896, NB, TOPK)
        kidx = [sb(f"kidx{i}", [P, NB, TOPK], U32) for i in range(2)]
        bidx = sb("bidx", [P, NB, TOPK], U32)
        part_u = sb("part_u", [P, NB, TOPK], U32)
        idx_next = sb("idx_next", [P, PICKS], U32)
        idx_cur = sb("idx_cur", [P, PICKS], U32)
        gate_cur = sb("gate_cur", [P, PICKS])
        sks = sb("sks", [P, 2, NKEYS])
        dots = sb("dots", [P, RING])
        gl = sb("gl", [P, 4])
        idg = sb("idg", [P, 4, P])
        dg = sb("dg", [P, 4, P])
        norm = sb("norm", [P, NB])
        cand = big[:].rearrange("p (b i j) -> p b i j", b=NB, i=TOPK)
        SPLIT = 96
        DVE_PER_TURN = 2 * NB * 4 + 1 + NB * 4 + 1 + 12 + 6 + 2

        Q_AT = (0, 20)
        S_AT = (18, 38)
        TOP_AT = (22, 44)
        CAND_AT, BEST_AT, DECODE_AT = 53, 54, 74

        with nc.Block() as block:
            @block.sync
            def _(sp):
                sp.dma_start(sks[:].rearrange("p a n -> p (a n)"), sk[0]).then_inc(in_wqn, 16)
                sp.wait_ge(x1_stored, 16 * NB)
                with sp.Fori(0, HEADS - 1) as t:
                    sp.wait_ge(s_mm, t * 2 + 2)
                    sp.dma_start(at(MODS, 2048), w_q[bass.ds(t + 1, 1)].rearrange("a p f -> (a p) f")).then_inc(in_wq, 16)
                    sp.dma_start(sks[:].rearrange("p a n -> p (a n)"), sk[bass.ds(t + 1, 1)].rearrange("a p f -> (a p) f")).then_inc(in_wqn, 16)

            @block.gpsimd
            def _(pool):
                pool.memset(at(R2, 8192), 0.0).then_inc(zeroed, 1)
                pool.wait_ge(x1_stored, 16 * NB)

                def gathers(t):
                    for n in range(PICKS):
                        if n in (0, SPLIT):
                            pool.wait_ge(published, t * 2 + (1 if n == 0 else 2))
                        pool.wait_ge(ring_free, t * PICKS + n + 1)
                        apart(pool, pool_steps)
                        pool.indirect_dma_start(ring[:, n % RING, :], None, uv,
                                                bass.IndirectOffsetOnAxis(ap=idx_cur[:, n:n + 1], axis=0)).then_inc(gathered[n % RING], 16)

                with pool.Fori(0, HEADS) as t:
                    gathers(t)

            @block.tensor
            def _(pe):
                def project(h, p, i):
                    half, k = i // KT, i % KT
                    if p == 0 and i == 0:
                        pe.wait_ge(in_wq, h * 16 + 16)
                        pe.wait_ge(in_wqn, h * 16 + 16)
                    if i == 0:
                        pe.wait_ge(q_taken, h * 4 + 2 * p)
                    m = pe.matmul(pb[:, half, :], wq[:, p, k, :], h2T[:, k, half * HALF:(half + 1) * HALF],
                                  start=(k == 0), stop=(k == KT - 1))
                    if k == KT - 1:
                        m.then_inc(q_mm, 1)

                def half_scores(h, p, b):
                    if b == 0:
                        pe.wait_ge(q_taken, h * 4 + 2 * p + 2)
                        pe.wait_ge(s_taken, h * 4 + 2 * p)
                    m = pe.matmul(pb[:, 2 + b // 4, (b % 4) * P:(b % 4 + 1) * P], qpT[:, b * P:(b + 1) * P], sks[:, p, :],
                                  start=True, stop=True)
                    if b == NB - 1:
                        m.then_inc(s_mm, 1)

                def turn(t, keys):
                    for n in range(PICKS):
                        if keys:
                            for p in range(2):
                                if Q_AT[p] <= n < Q_AT[p] + 16:
                                    project(t + 1, p, n - Q_AT[p])
                                if S_AT[p] <= n < S_AT[p] + 2:
                                    for b in range(4 * (n - S_AT[p]), 4 * (n - S_AT[p]) + 4):
                                        half_scores(t + 1, p, b)
                        b, k = n // TOPK, n % TOPK
                        if k == 0:
                            pe.wait_ge(acc_free, t * NB + b + 1)
                        pe.wait_ge(diag_done, LED + t * PICKS + n + 1)
                        for i in range(2):
                            m = pe.matmul(pb[:, 4 + 2 * (b % 2) + i, :], dg[:, n % 4, :],
                                          ring[:, n % RING, D + i * HALF:D + (i + 1) * HALF], start=(k == 0), stop=(k == TOPK - 1))
                        m.then_inc(ring_free, 1)

                pe.sem_inc(ring_free, RING)
                pe.sem_inc(acc_free, 2)
                for p in range(2):
                    for i in range(16):
                        project(0, p, i)
                    for b in range(NB):
                        half_scores(0, p, b)
                with pe.Fori(0, HEADS - 1) as t:
                    turn(t, True)
                turn(HEADS - 1, False)

            @block.scalar
            def _(act):
                def take_query(h, p, i):
                    act.wait_ge(q_mm, h * 4 + 2 * p + i + 1)
                    act.wait_ge(s_mm, h * 2 + p)
                    act.activation(qpT[:, i * HALF:(i + 1) * HALF], pb[:, i, :], ACT.Copy).then_inc(q_taken, 1)

                def take_scores(h, p):
                    act.wait_ge(s_mm, h * 2 + p + 1)
                    act.wait_ge(s_used, h * 2 + p)
                    for i in range(2):
                        act.activation(ssb[:, 4 * i:4 * i + 4, :].rearrange("p a b -> p (a b)"), pb[:, 2 + i, :], ACT.Copy).then_inc(s_taken, 1)

                def gate_exp(h):
                    act.wait_ge(picked, h + 1)
                    act.activation(best, best, ACT.Exp).then_inc(picked_exp, 1)

                def scaled_identity(t, n):
                    if n in (0, SPLIT):
                        act.wait_ge(published, t * 2 + (1 if n == 0 else 2))
                    act.wait_ge(diag_done, LED + t * PICKS + max(n - 3, 0))
                    act.activation(idg[:, n % 4, :], ident[:], ACT.Copy, scale=gate_cur[:, n:n + 1]).then_inc(idg_done, 1)

                def turn(t, keys):
                    for n in (0, 1):
                        scaled_identity(t, n)
                    for n in range(0, PICKS, 2):
                        for m in (n + 2, n + 3):
                            if m < PICKS:
                                scaled_identity(t, m)
                        act.wait_ge(dots_done, t * PICKS + n + 2)
                        act.wait_ge(diag_done, LED + t * PICKS + n)
                        act.activation(gl[:, 0:2], dots[:, n % RING:n % RING + 2], ACT.Gelu).then_inc(gelu_done, 1)
                        act.wait_ge(gelu_done, t * (PICKS // 2) + n // 2 + 1)
                        act.wait_ge(idg_done, t * PICKS + n + 2)
                        for m in (n, n + 1):
                            act.wait_ge(ring_free, t * PICKS + m - 3 + RING)
                            act.activation(dg[:, m % 4, :], idg[:, m % 4, :], ACT.Copy, scale=gl[:, m - n:m - n + 1]).then_inc(diag_done, 1)
                        if keys:
                            for p in range(2):
                                if n in (Q_AT[p] + 10, Q_AT[p] + 18 - 2):
                                    take_query(t + 1, p, 0 if n == Q_AT[p] + 10 else 1)
                                if n == S_AT[p] + 2:
                                    take_scores(t + 1, p)
                            if n == DECODE_AT + 16:
                                gate_exp(t + 1)

                lead(act, diag_done)
                for p in range(2):
                    for i in range(2):
                        take_query(0, p, i)
                    take_scores(0, p)
                gate_exp(0)
                with act.Fori(0, HEADS - 1) as t:
                    turn(t, True)
                turn(HEADS - 1, False)

            @block.vector
            def _(dve):
                link = Chain(dve, dve_p)

                def top16(values, indices, scores):
                    apart(dve, dve_steps)
                    link(dve.max(values[:, 0:8], scores))
                    apart(dve, dve_steps)
                    link(dve.max_index(indices[:, 0:8], values[:, 0:8], scores))
                    apart(dve, dve_steps)
                    link(dve.match_replace(scores, values[:, 0:8], scores, LOWEST))
                    apart(dve, dve_steps)
                    link(dve.max(values[:, 8:16], scores))
                    apart(dve, dve_steps)
                    return dve.max_index(indices[:, 8:16], values[:, 8:16], scores)

                def top_half(h, p, b):
                    if b == 0:
                        dve.wait_ge(s_taken, h * 4 + 2 * p + 2)
                    op = top16(vals[p][:, b, :], kidx[p][:, b, :], ssb[:, b, :])
                    if b == NB - 1:
                        op.then_inc(s_used, 1)

                def candidates(h):
                    dve.wait_ge(s_used, h * 2 + 2)
                    link(dve.tensor_tensor(cand, vals[0].unsqueeze(3).to_broadcast([P, NB, TOPK, TOPK]),
                                           vals[1].unsqueeze(2).to_broadcast([P, NB, TOPK, TOPK]), ALU.add))

                def top_pairs(h, b):
                    op = top16(best[:, b, :], bidx[:, b, :], cand[:, b].rearrange("p i j -> p (i j)"))
                    if b == NB - 1:
                        link(op)

                def decode(h, step):
                    p = 0 if step < 6 else 1
                    wide = cand.rearrange("p b k i -> p (b k) i")
                    f = fl[p].rearrange("p b k -> p (b k)")
                    q = step % 6
                    if step < 12 and q == 0:
                        if p == 0:
                            link(dve.tensor_scalar(part_u[:], bidx[:], 4, None, ALU.logical_shift_right))
                        else:
                            link(dve.tensor_scalar(part_u[:], bidx[:], TOPK - 1, None, ALU.bitwise_and))
                    elif step < 12 and q == 1:
                        link(dve.tensor_copy(f, part_u[:].rearrange("p b k -> p (b k)")))
                    elif step < 12 and q == 2:
                        link(dve.tensor_tensor(wide, f.unsqueeze(2).to_broadcast([P, PICKS, TOPK]),
                                               iota16[:].unsqueeze(1).to_broadcast([P, PICKS, TOPK]), ALU.is_equal))
                    elif step < 12 and q == 3:
                        link(dve.tensor_copy(fl[p], kidx[p][:]))
                    elif step < 12 and q == 4:
                        link(dve.tensor_tensor(cand, cand, fl[p].unsqueeze(2).to_broadcast([P, NB, TOPK, TOPK]), ALU.mult))
                    elif step < 12:
                        link(dve.tensor_reduce(res[p].rearrange("p b k -> p (b k)"), wide, AX, ALU.add))
                    elif step == 12:
                        link(dve.scalar_tensor_tensor(out=res[0], in0=res[0], scalar=float(NKEYS), in1=res[1], op0=ALU.mult, op1=ALU.add))
                        link(dve.tensor_copy(idx_next[:], res[0].rearrange("p b k -> p (b k)")))
                        link(dve.tensor_copy(norm[:], best[:, :, 0]))
                        dve.tensor_tensor(best, best, norm[:].unsqueeze(2).to_broadcast([P, NB, TOPK]), ALU.subtract).then_inc(picked, 1)
                    else:
                        dve.wait_ge(picked_exp, h + 1)
                        link(dve.tensor_reduce(norm[:], best, AX, ALU.add))
                        link(dve.reciprocal(norm[:], norm[:]))
                        link(dve.tensor_tensor(gate_next, best, norm[:].unsqueeze(2).to_broadcast([P, NB, TOPK]), ALU.mult))

                def publish(a, b, before):
                    if before is not None:
                        dve.wait_ge(diag_done, LED + before)
                    link(dve.tensor_copy(idx_cur[:, a:b], idx_next[:, a:b]))
                    dve.tensor_copy(gate_cur[:, a:b], gate_next.rearrange("p b k -> p (b k)")[:, a:b]).then_inc(published, 1)

                def add_block(t, b):
                    dve.wait_ge(ring_free, t * PICKS + b * TOPK + TOPK + RING)
                    dve.wait_ge(acc_free, t * NB + b + 2)
                    dve.tensor_tensor(acc[:, b, :], acc[:, b, :], pb[:, 4 + 2 * (b % 2):6 + 2 * (b % 2), :].rearrange("p a b -> p (a b)"),
                                      ALU.add).then_inc(acc_free, 1)

                def turn(t, keys):
                    for n in range(PICKS):
                        b = n // TOPK
                        dve.wait_ge(gathered[n % RING], t * (PICKS // RING * 16) + 16 * (n // RING) + 16)
                        u = ring[:, n % RING, 0:D]
                        dve.tensor_tensor_reduce(u, h2[:, b, :], u, 1.0, 0.0, ALU.mult, ALU.add,
                                                 dots[:, n % RING:n % RING + 1]).then_inc(dots_done, 1)
                        if b and n % TOPK == 4:
                            add_block(t, b - 1)
                        if keys:
                            for p in range(2):
                                if TOP_AT[p] <= n < TOP_AT[p] + NB:
                                    top_half(t + 1, p, n - TOP_AT[p])
                            if n == CAND_AT:
                                candidates(t + 1)
                            if BEST_AT <= n < BEST_AT + 2 * NB and (n - BEST_AT) % 2 == 0:
                                top_pairs(t + 1, (n - BEST_AT) // 2)
                            if DECODE_AT <= n < DECODE_AT + 13:
                                decode(t + 1, n - DECODE_AT)
                            if n == DECODE_AT + 22:
                                decode(t + 1, 13)
                            if n == PICKS - 12:
                                publish(0, SPLIT, t * PICKS + SPLIT)
                    if keys:
                        publish(SPLIT, PICKS, t * PICKS + PICKS)
                    add_block(t, NB - 1)

                dve.wait_ge(zeroed, 1)
                for p in range(2):
                    for b in range(NB):
                        top_half(0, p, b)
                candidates(0)
                for b in range(NB):
                    top_pairs(0, b)
                for step in range(14):
                    decode(0, step)
                publish(0, SPLIT, None)
                publish(SPLIT, PICKS, None)
                with dve.Fori(0, HEADS - 1) as t:
                    before = link.n
                    link.enter(t, DVE_PER_TURN)
                    turn(t, True)
                    link.leave(HEADS - 1)
                turn(HEADS - 1, False)

        in_x1 = [sem(f"in_x1_{b}") for b in range(NB)]
        in_gf = sem("in_gf")
        f_sum = sem("f_sum")
        f_square = sem("f_square")
        f_rinv = sem("f_rinv")
        f_rstd = sem("f_rstd")
        f_done = sem("f_done")
        f_own = sem("f_own")
        out_stored = sem("out_stored")
        final_g = at(MODS, D)
        xf = rows(R3, NB, D)
        junk = at(MODS + D, D)

        with nc.Block() as block:
            @block.sync
            def _(sp):
                sp.dma_start(final_g, gf.partition_broadcast(P)).then_inc(in_gf, 16)
                for b in range(NB):
                    sp.dma_start(xf[:, b, :], x1_dram[b * P:(b + 1) * P, :]).then_inc(in_x1[b], 16)
                for b in range(NB):
                    sp.wait_ge(f_done, b + 1)
                    sp.dma_start(out[b * P:(b + 1) * P, :], acc[:, b, :]).then_inc(out_stored, 16)
                sp.wait_ge(out_stored, 16 * NB)

            @block.scalar
            def _(act):
                for b in range(NB):
                    act.wait_ge(f_sum, b + 1)
                    act.wait_ge(f_square, b)
                    act.activation(junk, acc[:, b, :], ACT.Square, accum_out=stats[:, b:b + 1]).then_inc(f_square, 1)
                    act.wait_ge(f_rinv, b + 1)
                    act.activation(stats[:, 16 + b:17 + b], stats[:, 8 + b:9 + b], ACT.Sqrt).then_inc(f_rstd, 1)

            @block.vector
            def _(dve):
                link = Chain(dve, f_own)

                def residual(b):
                    link(dve.tensor_tensor(acc[:, b, :], acc[:, b, :], mod(GATE2), ALU.mult))
                    dve.wait_ge(in_x1[b], 16)
                    dve.tensor_tensor(acc[:, b, :], acc[:, b, :], xf[:, b, :], ALU.add).then_inc(f_sum, 1)

                dve.wait_ge(in_gf, 16)
                residual(0)
                for b in range(NB):
                    if b + 1 < NB:
                        residual(b + 1)
                    dve.wait_ge(f_square, b + 1)
                    link(dve.tensor_scalar(stats[:, 24 + b:25 + b], stats[:, b:b + 1], 1.0 / D, EPS, ALU.mult, ALU.add))
                    dve.reciprocal(stats[:, 8 + b:9 + b], stats[:, 24 + b:25 + b]).then_inc(f_rinv, 1)
                    dve.wait_ge(f_rstd, b + 1)
                    dve.scalar_tensor_tensor(out=acc[:, b, :], in0=acc[:, b, :], scalar=stats[:, 16 + b:17 + b],
                                             in1=final_g, op0=ALU.mult, op1=ALU.mult).then_inc(f_done, 1)


def shape_constants():
    j, s = np.mgrid[0:P, 0:P]
    tri = -(j >= s).astype(np.float32)
    t, k = np.mgrid[0:P, 0:BAND]
    key = k - CHUNK
    behind = t // CHUNK - key // CHUNK
    seen = (behind == 0) | (behind == 1)
    slopes = 2.0 ** (-8.0 * np.arange(1, SW_HEADS + 1) / SW_HEADS)
    table = np.where(seen[:, None, :], -slopes[None, :, None] * np.abs(t - key)[:, None, :], -1e30)
    iota = np.broadcast_to(np.arange(TOPK, dtype=np.float32), (P, TOPK))
    unseen = np.where(j >= s, -1e30, 0.0)
    return np.concatenate([np.eye(P), tri, iota, table.reshape(P, -1), unseen], axis=1).astype(np.float32)


def kernel(**inputs):
    import concourse.bacc as _bacc
    from concourse.bass_utils import run_bass_kernel_spmd as _run

    a = {k: np.asarray(v) for k, v in inputs.items()}
    w_in = a["w_in"][0]
    sbw = SB_PAIRS * P
    w_sb = w_in[:, :3 * sbw].reshape(KT, P, 3, SB_PAIRS, P).transpose(3, 1, 2, 0, 4).reshape(SB_PAIRS, P, -1)
    o = 3 * sbw
    wq = w_in[:, o:o + 512].reshape(KT, P, 2, 4, DH).transpose(1, 3, 0, 2, 4).reshape(P, 4, KT, P)
    wkv = w_in[:, o + 512:o + 768].reshape(KT, P, 2, P).transpose(1, 2, 0, 3)
    w_sw = np.concatenate([wq, wkv], axis=1).reshape(P, -1)
    gates = w_in[:, o + 768:].reshape(KT, P, 2, KT, P).transpose(3, 1, 2, 0, 4).reshape(KT, P, 2 * KT, P)
    p_sb = a["sb_proj"][0].reshape(4, P, KT, P).transpose(2, 1, 0, 3)
    p_sw = a["sw_proj"][0].reshape(2, 4, DH, D).transpose(1, 0, 2, 3).reshape(4, P, KT, P).transpose(2, 1, 0, 3)
    arrays = {
        "x": a["x"][0],
        "c8": a["c"].reshape(KT, P).T,
        "w_ada": a["w_ada"][0].reshape(KT, P, 12, HALF).transpose(2, 1, 0, 3),
        "b_ada": a["b_ada"],
        "g1": a["norm1_g"][0],
        "g2": a["norm2_g"][0],
        "gf": a["final_g"],
        "w_sb": w_sb,
        "w_sw": w_sw,
        "sinks": a["sw_sinks"][0],
        "w_mg": np.concatenate([gates, p_sb, p_sw], axis=2).reshape(KT, P, -1),
        "w_out": a["w_out"][0].reshape(KT, P, D).transpose(1, 0, 2).reshape(P, -1),
        "w_q": a["peer_wq"][0].reshape(KT, P, HEADS, 2, P).transpose(2, 1, 3, 0, 4).reshape(HEADS, P, -1),
        "sk": a["peer_sub_keys"][0].transpose(0, 3, 1, 2).reshape(HEADS, P, -1),
        "uv": np.concatenate([a["peer_u"][0], a["peer_v"][0]], axis=1),
        "consts": shape_constants(),
    }
    arrays = {k: np.ascontiguousarray(v) for k, v in arrays.items()}
    nc = _bacc.Bacc("TRN2", target_bir_lowering=False, num_devices=1)
    args = [nc.dram_tensor("in_" + k, v.shape, mybir.dt.from_np(v.dtype), kind="ExternalInput").ap() for k, v in arrays.items()]
    args.append(nc.dram_tensor("x1_scratch", (S, D), F32, kind="Internal").ap())
    args.append(nc.dram_tensor("out_0", (S, D), F32, kind="ExternalOutput").ap())
    build(nc, *args)
    r = _run(nc, [{"in_" + k: v for k, v in arrays.items()}], core_ids=[0])
    return r.results[0]["out_0"].reshape(1, S, D)
```

```python
from contextlib import ExitStack

import numpy as np

import concourse.bass as bass
from concourse import mybir

F32 = mybir.dt.float32
U32 = mybir.dt.uint32
BF16 = mybir.dt.bfloat16
ALU = mybir.AluOpType
ACT = mybir.ActivationFunctionType
AX = mybir.AxisListType.X

P = 128
D = 1024
S = 1024
KT = D // P
NB = S // P
HALF = 512
DH = 64
SCALE = DH ** -0.5
SB_PAIRS = 4
SW_HEADS = 8
CHUNK = 64
BAND = 3 * CHUNK
HEADS = 8
NKEYS = 128
TOPK = 16
PICKS = NB * TOPK
RING = 8
EPS = 1e-6
LOWEST = -3.0e38
EXP_LN_TABLES = 6
LED = 1

HT = 0
R4 = 8192
R2 = 16384
R3 = 24576
R1 = 32768
MODS = 40960
ARENA = MODS + 6 * D
SHIFT1, SCALE1, GATE1, SHIFT2, SCALE2, GATE2 = range(6)


class Chain:

    def __init__(self, eng, sem):
        self.eng, self.sem, self.n, self.turn, self.per = eng, sem, 0, None, 0

    def __call__(self, ins):
        ins.then_inc(self.sem, 1)
        self.n += 1
        more = 0 if self.turn is None else self.turn * self.per
        self.eng.wait_ge(self.sem, more + self.n)

    def enter(self, turn, per):
        self.turn, self.per, self.at = turn, per, self.n

    def leave(self, turns):
        assert self.n - self.at == self.per, (self.n - self.at, self.per)
        self.n = self.at + turns * self.per
        self.turn = None


def apart(eng, steps):
    eng.sem_inc(steps, 1)


def lead(eng, *semaphores):
    for s in semaphores:
        eng.sem_inc(s, LED)


def load_exp_ln_tables(nc, act):
    act.add_instruction(mybir.InstLoadActFuncSet(name=nc.get_next_instruction_name(), act_func_set_id=EXP_LN_TABLES,
                                                 engine=mybir.EngineType.Activation, ins=[], outs=[]))


def stick_chunks():
    out = []
    for e in range(2):
        for s in reversed(range(NB)):
            cuts = [(HALF, S), (s * P, HALF)] if s < 4 else [(s * P, S)]
            out += [(e, s, lo, hi) for lo, hi in cuts]
    return out


def build(nc, x, c8, w_ada, b_ada, g1, g2, gf, w_sb, w_sw, sinks, w_mg, w_out, w_q, sk, uv, consts, x1_dram, out):
    with ExitStack() as ctx:
        def sb(name, shape, dt=F32):
            return ctx.enter_context(nc.sbuf_tensor(name, shape, dt))

        def sem(name):
            return ctx.enter_context(nc.semaphore(name))

        arena = sb("arena", [P, ARENA])
        ident = sb("ident", [P, P])
        tri = sb("tri", [P, P])
        negones = sb("negones", [P, P])
        ident_b = sb("ident_b", [P, P], BF16)
        unseen_b = sb("unseen_b", [P, P], BF16)
        iota16 = sb("iota16", [P, TOPK])
        big = sb("big", [P, 2048])
        stats = sb("stats", [P, 32])
        sink_row = sb("sink_row", [P, SW_HEADS])
        small = sb("small", [P, 64])
        pb = ctx.enter_context(nc.psum_tensor("pb", [P, 8, HALF], F32))

        def at(off, n):
            return arena[:, off:off + n]

        def mod(v):
            return at(MODS + v * D, D)

        def rows(off, a, b):
            return at(off, a * b).rearrange("p (a b) -> p a b", a=a)

        hT = rows(HT, KT, S)

        dve_steps = sem("dve_steps")
        pool_steps = sem("pool_steps")
        in_small = sem("in_small")
        in_consts = sem("in_consts")
        in_rows = sem("in_rows")
        in_bias = sem("in_bias")
        in_x = sem("in_x")
        in_ada = [sem(f"in_ada{i}") for i in range(4)]
        in_wsb = sem("in_wsb")
        in_wsw = sem("in_wsw")
        sig_c = sem("sig_c")
        c_wide = sem("c_wide")
        ada_mm = sem("ada_mm")
        ada_act = sem("ada_act")
        ada_dve = sem("ada_dve")
        sq_done = sem("sq_done")
        rinv = sem("rinv")
        rstd_done = sem("rstd_done")
        h_done = sem("h_done")
        tr_done = sem("tr_done")
        tr_act = sem("tr_act")
        tr_dve = sem("tr_dve")
        dve_own = sem("dve_own")
        wada = rows(R4, 4, 4096)
        cb = rows(R1, KT, P)
        brow = arena[0:1, R1 + 1024:R1 + 1024 + 6 * D]
        xt = rows(R3, NB, D)
        chain_at = [0]
        TABLE = SW_HEADS * BAND
        DVE_HALVES = (2, 3, 8, 9)

        def evacuations(j):
            mine = [i for i in range(12) if (i in DVE_HALVES) == (j in DVE_HALVES)]
            return (ada_dve if j in DVE_HALVES else ada_act), mine.index(j) + 1

        with nc.Block() as block:
            @block.sync
            def _(sp):
                sp.dma_start(small[:, 0:KT], c8).then_inc(in_small, 16)
                sp.dma_start(brow, b_ada).then_inc(in_bias, 16)
                for j in range(4):
                    sp.dma_start(wada[:, j, :], w_ada[j].rearrange("p k n -> p (k n)")).then_inc(in_ada[j % 4], 16)
                    if j == 1:
                        sp.dma_start(xt, x.rearrange("(b p) d -> p b d", p=P)).then_inc(in_x, 16)
                sp.dma_start(mod(SCALE1), g1.partition_broadcast(P)).then_inc(in_rows, 16)
                sp.dma_start(mod(SCALE2), g2.partition_broadcast(P)).then_inc(in_rows, 16)
                sp.dma_start(sink_row[:], sinks.partition_broadcast(P)).then_inc(in_rows, 16)
                for j in range(4, 12):
                    sp.wait_ge(ada_mm, j - 3)
                    sp.dma_start(wada[:, j % 4, :], w_ada[j].rearrange("p k n -> p (k n)")).then_inc(in_ada[j % 4], 16)
                sp.wait_ge(ada_mm, 9)
                sp.dma_start(at(R4, 3072), w_sb[0]).then_inc(in_wsb, 16)
                sp.wait_ge(ada_mm, 12)
                sp.dma_start(at(R2, 6144), w_sw).then_inc(in_wsw, 16)

            @block.gpsimd
            def _(pool):
                pool.dma_start(ident[:], consts[:, 0:P]).then_inc(in_consts, 16)
                pool.dma_start(tri[:], consts[:, P:2 * P]).then_inc(in_consts, 16)
                pool.dma_start(iota16[:], consts[:, 2 * P:2 * P + TOPK]).then_inc(in_consts, 16)
                pool.dma_start(big[:, 0:TABLE + P], consts[:, 2 * P + TOPK:2 * P + TOPK + TABLE + P]).then_inc(in_consts, 16)

            @block.scalar
            def _(act):
                act.wait_ge(in_small, 16)
                act.activation(small[:, 8:16], small[:, 0:8], ACT.Sigmoid).then_inc(sig_c, 1)
                act.wait_ge(in_x, 16)
                for b in range(NB):
                    act.wait_ge(sq_done, b)
                    act.activation(pb[:, 4:6, :].rearrange("p a b -> p (a b)"), xt[:, b, :], ACT.Square,
                                   accum_out=stats[:, b:b + 1]).then_inc(sq_done, 1)
                for j in (0, 1):
                    act.wait_ge(ada_mm, j + 1)
                    act.activation(mod(SHIFT1)[:, j * HALF:(j + 1) * HALF], pb[:, j % 4, :], ACT.Copy).then_inc(ada_act, 1)
                act.wait_ge(rinv, 1)
                act.activation(stats[:, 16:24], stats[:, 8:16], ACT.Sqrt).then_inc(rstd_done, 1)
                for b in range(NB):
                    act.wait_ge(tr_done, 2 * b + 1)
                    act.activation(hT[:, 0:4, b * P:(b + 1) * P], pb[:, 4 + 2 * (b % 2), :].rearrange("p (a b) -> p a b", a=4),
                                   ACT.Copy).then_inc(tr_act, 1)
                    j = 4 + b
                    if j not in DVE_HALVES:
                        act.wait_ge(ada_mm, j + 1)
                        act.activation(mod(j // 2)[:, (j % 2) * HALF:(j % 2 + 1) * HALF], pb[:, j % 4, :],
                                       ACT.Copy).then_inc(ada_act, 1)

            @block.vector
            def _(dve):
                link = Chain(dve, dve_own)

                def scale_half(j):
                    dve.wait_ge(ada_mm, j + 1)
                    row = mod(j // 2)[:, (j % 2) * HALF:(j % 2 + 1) * HALF]
                    dve.scalar_tensor_tensor(out=row, in0=pb[:, j % 4, :], scalar=1.0, in1=row, op0=ALU.add,
                                             op1=ALU.mult).then_inc(ada_dve, 1)

                link(dve.memset(small[:, 32:33], 1.0))
                dve.wait_ge(sig_c, 1)
                link(dve.tensor_tensor(small[:, 16:24], small[:, 0:8], small[:, 8:16], ALU.mult))
                dve.tensor_copy(cb, small[:, 16:24].unsqueeze(2).to_broadcast([P, KT, P])).then_inc(c_wide, 1)
                dve.memset(negones[:], -1.0)
                dve.wait_ge(in_consts, 64)
                dve.tensor_copy(ident_b[:], ident[:])
                dve.tensor_copy(unseen_b[:], big[:, TABLE:TABLE + P])
                dve.wait_ge(sq_done, NB)
                link(dve.tensor_scalar(stats[:, 24:32], stats[:, 0:8], 1.0 / D, EPS, ALU.mult, ALU.add))
                dve.reciprocal(stats[:, 8:16], stats[:, 24:32]).then_inc(rinv, 1)
                dve.wait_ge(in_rows, 48)
                scale_half(2)
                scale_half(3)
                dve.wait_ge(ada_dve, 2)
                dve.wait_ge(ada_act, 2)
                dve.wait_ge(rstd_done, 1)
                for b in range(NB):
                    link(dve.scalar_tensor_tensor(out=xt[:, b, :], in0=xt[:, b, :], scalar=stats[:, 16 + b:17 + b],
                                                  in1=mod(SCALE1), op0=ALU.mult, op1=ALU.mult))
                    dve.tensor_tensor(xt[:, b, :], xt[:, b, :], mod(SHIFT1), ALU.add).then_inc(h_done, 1)
                    if b:
                        a = b - 1
                        dve.wait_ge(tr_done, 2 * a + 2)
                        dve.tensor_copy(hT[:, 4:8, a * P:(a + 1) * P],
                                        pb[:, 5 + 2 * (a % 2), :].rearrange("p (a b) -> p a b", a=4)).then_inc(tr_dve, 1)
                    if b and 3 + b in DVE_HALVES:
                        scale_half(3 + b)
                a = NB - 1
                dve.wait_ge(tr_done, 2 * a + 2)
                dve.tensor_copy(hT[:, 4:8, a * P:(a + 1) * P],
                                pb[:, 5 + 2 * (a % 2), :].rearrange("p (a b) -> p a b", a=4)).then_inc(tr_dve, 1)
                chain_at[0] = link.n

            @block.tensor
            def _(pe):
                def modulation_half(j):
                    pe.wait_ge(in_ada[j % 4], 16 * (j // 4 + 1))
                    if j >= 4:
                        pe.wait_ge(*evacuations(j - 4))
                    w = wada[:, j % 4, :].rearrange("p (k n) -> p k n", k=KT)
                    for k in range(KT):
                        pe.matmul(pb[:, j % 4, :], cb[:, k, :], w[:, k, :], start=(k == 0), stop=False)
                    pe.matmul(pb[:, j % 4, :], small[0:1, 32:33].to_broadcast([1, P]), brow[:, j * HALF:(j + 1) * HALF],
                              start=False, stop=True).then_inc(ada_mm, 1)

                pe.wait_ge(c_wide, 1)
                pe.wait_ge(in_bias, 16)
                for j in range(4):
                    modulation_half(j)
                pe.wait_ge(in_consts, 64)
                for b in range(NB):
                    pe.wait_ge(h_done, b + 1)
                    if b < 2:
                        pe.wait_ge(sq_done, NB)
                    else:
                        pe.wait_ge(tr_act, b - 1)
                        pe.wait_ge(tr_dve, b - 1)
                    for k in range(KT):
                        t = pe.transpose(pb[:, 4 + 2 * (b % 2) + k // 4, (k % 4) * P:(k % 4 + 1) * P],
                                         xt[:, b, k * P:(k + 1) * P], ident[:])
                        if k % 4 == 3:
                            t.then_inc(tr_done, 1)
                    modulation_half(4 + b)

        chunks = stick_chunks()
        NC = len(chunks)
        proj = sem("proj")
        proj_act = sem("proj_act")
        proj_dve = sem("proj_dve")
        z_done = sem("z_done")
        abs_done = sem("abs_done")
        relu_done = sem("relu_done")
        e1_done = sem("e1_done")
        ln_done = sem("ln_done")
        sp_done = sem("sp_done")
        sums_done = sem("sums_done")
        att_done = sem("att_done")
        later_done = sem("later_done")
        pv_done = sem("pv_done")
        y_taken = sem("y_taken")
        dve_sb = sem("dve_sb")
        wsb = at(R4, 3072).rearrange("p (a k f) -> p a k f", a=3, k=KT)
        later = [at(R4 + 3072, S), at(R4 + 4096, S), at(R3 + 7168, S)]
        qT, kT = at(R1, S), at(R1 + S, S)
        v = rows(R1 + 2 * S, NB, P)
        AHEAD = 4
        DEEP = 6
        ZBANKS = 6
        zabs = rows(R1 + 3072, DEEP, HALF)
        spl = rows(R3 + 4096, DEEP, HALF)
        attn = rows(R4 + 5120, DEEP, HALF)

        def buf(ring, c, n):
            return ring[:, c % DEEP, 0:n]

        ysbT = rows(R3, SB_PAIRS, S)
        yswT = rows(R3 + 4096, SB_PAIRS, S)

        with nc.Block() as block:
            @block.sync
            def _(sp):
                with sp.Fori(0, SB_PAIRS - 1) as t:
                    sp.wait_ge(proj, t * 6 + 6)
                    sp.dma_start(at(R4, 3072), w_sb[bass.ds(t + 1, 1)].rearrange("a p f -> (a p) f")).then_inc(in_wsb, 16)

            @block.scalar
            def _(act):
                lead(act, att_done, y_taken)
                load_exp_ln_tables(nc, act)
                with act.Fori(0, SB_PAIRS) as t:
                    for i, dst in enumerate((qT, qT, kT, kT)):
                        act.wait_ge(proj, t * 6 + i + 1)
                        act.activation(dst[:, (i % 2) * HALF:(i % 2 + 1) * HALF], pb[:, i, :], ACT.Copy,
                                       scale=SCALE if i < 2 else 1.0).then_inc(proj_act, 1)

                    def softplus_log(c):
                        n = chunks[c][3] - chunks[c][2]
                        a = buf(zabs, c, n)
                        act.wait_ge(abs_done, t * NC + c + 1)
                        act.activation(a, a, ACT.Exp).then_inc(e1_done, 1)
                        act.wait_ge(e1_done, t * NC + c + 1)
                        act.activation(a, a, ACT.Ln, bias=1.0).then_inc(ln_done, 1)

                    for c in range(AHEAD):
                        softplus_log(c)
                    for c, (e, s, lo, hi) in enumerate(chunks):
                        act.wait_ge(sums_done, LED + t * NC + c + 1)
                        act.wait_ge(pv_done, LED + t * NC + max(c - DEEP + 1, 0))
                        act.activation(buf(attn, c, hi - lo), pb[:, c % ZBANKS, 0:hi - lo], ACT.Exp).then_inc(att_done, 1)
                        if c + AHEAD < NC:
                            softplus_log(c + AHEAD)
                    act.wait_ge(pv_done, LED + t * NC + NC)
                    for i in range(2):
                        act.activation(ysbT[:, bass.ds(t, 1), i * HALF:(i + 1) * HALF].rearrange("p a b -> p (a b)"),
                                       pb[:, 6 + i, :], ACT.Copy).then_inc(y_taken, 1)

            @block.vector
            def _(dve):
                lead(dve, proj_dve, sp_done, later_done)
                with dve.Fori(0, SB_PAIRS) as t:
                    def take_values(i):
                        dve.wait_ge(proj, t * 6 + 5 + i)
                        dve.tensor_copy(v[:, 4 * i:4 * i + 4, :].rearrange("p a b -> p (a b)"), pb[:, 4 + i, :]).then_inc(proj_dve, 1)

                    take_values(0)

                    def positive(c):
                        n = chunks[c][3] - chunks[c][2]
                        dve.wait_ge(z_done, t * NC + c + 1)
                        dve.wait_ge(sums_done, LED + t * NC + max(c - DEEP + 1, 0))
                        dve.wait_ge(later_done, LED + t * NC + max(c - DEEP + 1, 0))
                        dve.tensor_scalar(buf(spl, c, n), pb[:, c % ZBANKS, 0:n], 0.0, None, ALU.max).then_inc(relu_done, 1)

                    def magnitude(c):
                        n = chunks[c][3] - chunks[c][2]
                        dve.wait_ge(relu_done, t * NC + c + 1)
                        dve.scalar_tensor_tensor(out=buf(zabs, c, n), in0=buf(spl, c, n), scalar=-2.0,
                                                 in1=pb[:, c % ZBANKS, 0:n], op0=ALU.mult, op1=ALU.add).then_inc(abs_done, 1)

                    for c in range(AHEAD):
                        positive(c)
                        magnitude(c)
                    take_values(1)
                    for c, (e, s, lo, hi) in enumerate(chunks):
                        n = hi - lo
                        dve.wait_ge(ln_done, t * NC + c + 1)
                        dve.tensor_tensor(buf(spl, c, n), buf(spl, c, n), buf(zabs, c, n), ALU.add).then_inc(sp_done, 1)
                        if c + AHEAD < NC:
                            positive(c + AHEAD)
                        readers = [i + 1 for i, k in enumerate(chunks[:c]) if (k[1] + 1) % 3 == s % 3]
                        dve.wait_ge(sums_done, LED + t * NC + max(readers, default=0))
                        dve.wait_ge(sp_done, LED + t * NC + c + 1)
                        dve.wait_ge(later_done, LED + t * NC + c)
                        own = lo == s * P
                        if own:
                            op = dve.tensor_copy(later[s % 3][:, lo:lo + P], buf(spl, c, P))
                        a = lo + P if own else lo
                        if a < hi:
                            op = dve.tensor_tensor(later[s % 3][:, a:hi], later[(s + 1) % 3][:, a:hi],
                                                   buf(spl, c, n)[:, a - lo:n], ALU.add)
                        op.then_inc(later_done, 1)
                        if c + AHEAD < NC:
                            magnitude(c + AHEAD)

            @block.tensor
            def _(pe):
                lead(pe, sums_done, pv_done)
                with pe.Fori(0, SB_PAIRS) as t:
                    pe.wait_ge(in_wsb, t * 16 + 16)
                    pe.wait_ge(att_done, LED + t * NC)
                    for i in range(4):
                        for k in range(KT):
                            m = pe.matmul(pb[:, i, :], wsb[:, i // 2, k, :], hT[:, k, (i % 2) * HALF:(i % 2 + 1) * HALF],
                                          start=(k == 0), stop=(k == KT - 1))
                        m.then_inc(proj, 1)
                    pe.wait_ge(proj_dve, LED + t * 2)

                    def project_values(half):
                        for b in range(4):
                            for k in range(KT):
                                m = pe.matmul(pb[:, 4 + half, b * P:(b + 1) * P], hT[:, k, half * HALF + b * P:half * HALF + (b + 1) * P],
                                              wsb[:, 2, k, :], start=(k == 0), stop=(k == KT - 1))
                        m.then_inc(proj, 1)

                    def scores(c):
                        e, s, lo, hi = chunks[c]
                        pe.wait_ge(att_done, LED + t * NC + max(c - ZBANKS + 1, 0))
                        m = pe.matmul(pb[:, c % ZBANKS, 0:hi - lo], kT[64 * e:64 * e + 64, s * P:(s + 1) * P],
                                      qT[64 * e:64 * e + 64, lo:hi], start=True, stop=True)
                        if lo == s * P:
                            m = pe.matmul(pb[:, c % ZBANKS, 0:P], ident_b[:], unseen_b[:], start=False, stop=True,
                                          skip_group_check=True)
                        m.then_inc(z_done, 1)

                    def values(c):
                        e, s, lo, hi = chunks[c]
                        pe.wait_ge(att_done, LED + t * NC + c + 1)
                        bank = 6 + lo // HALF
                        pe.matmul(pb[64 * e:64 * e + 64, bank, lo % HALF:lo % HALF + hi - lo], v[:, s, 64 * e:64 * e + 64],
                                  buf(attn, c, hi - lo), start=s == (7 if lo >= HALF else 3), stop=s == 0,
                                  skip_group_check=True).then_inc(pv_done, 1)

                    project_values(0)
                    pe.wait_ge(proj_act, t * 4 + 4)
                    for c in range(AHEAD):
                        scores(c)
                    project_values(1)
                    pe.wait_ge(proj_dve, LED + t * 2 + 1)
                    scores(AHEAD)
                    pe.wait_ge(proj_dve, LED + t * 2 + 2)
                    for c, (e, s, lo, hi) in enumerate(chunks):
                        a = max(lo, (s + 1) * P)
                        pe.wait_ge(sp_done, LED + t * NC + c + 1)
                        m = pe.matmul(pb[:, c % ZBANKS, 0:hi - lo], tri[:], buf(spl, c, hi - lo), start=False,
                                      stop=True, skip_group_check=True)
                        if a < hi:
                            behind = max(i for i, k in enumerate(chunks) if k[:2] == (e, s + 1) and k[2] < hi and k[3] > a)
                            pe.wait_ge(later_done, LED + t * NC + behind + 1)
                            m = pe.matmul(pb[:, c % ZBANKS, a - lo:hi - lo], negones[:], later[(s + 1) % 3][:, a:hi],
                                          start=False, stop=True, skip_group_check=True)
                        m.then_inc(sums_done, 1)
                        if c + ZBANKS - 1 < NC:
                            scores(c + ZBANKS - 1)
                        if c == 0:
                            pe.wait_ge(y_taken, LED + t * 2)
                        else:
                            values(c - 1)
                    values(NC - 1)

        sw_proj_done = sem("sw_proj_done")
        sw_act = sem("sw_act")
        sw_dve = sem("sw_dve")
        sc_done = sem("sc_done")
        biased = sem("biased")
        shifted = sem("shifted")
        exp_done = sem("exp_done")
        probs_done = sem("probs_done")
        peaked = sem("peaked")
        summed = sem("summed")
        pt_done = sem("pt_done")
        pt_act = sem("pt_act")
        ysw_done = sem("ysw_done")
        ysw_taken = sem("ysw_taken")
        dve_sw = sem("dve_sw")
        pool_sw = sem("pool_sw")
        in_wq = sem("in_wq")
        wsw = rows(R2, 6 * KT, P).rearrange("p (a k) f -> p a k f", a=6)
        qb = rows(R1, 4, S)
        kb = at(R1 + 4096, S)
        vb = rows(R1 + 5120, NB, P)
        prob = at(R1 + 6144, 2048).rearrange("p (h n) -> p h n", h=SW_HEADS)
        SCB = 3
        sc2 = rows(R4, SCB, SW_HEADS * BAND)
        pT = at(R4 + 4608, 2048).rearrange("p (h w t) -> p h w t", h=SW_HEADS, w=2)
        peak = rows(R4 + 6656, SCB, 8)
        sink_e = rows(R4 + 6688, SCB, 8)
        total = rows(R4 + 6720, SCB, 8)
        in_wmg = sem("in_wmg")

        with nc.Block() as block:
            @block.sync
            def _(sp):
                sp.dma_start(at(MODS, 2048), w_q[0]).then_inc(in_wq, 16)

            def part(b):
                off = CHUNK if b == 0 else 0
                return sc2[:, b % SCB, :].rearrange("p (h n) -> p h n", h=SW_HEADS)[:, :, off:], BAND - off

            @block.gpsimd
            def _(pool):
                pool.memset(prob[:, :, 0:CHUNK], 0.0).then_inc(pool_sw, 1)

                def shift(b):
                    s, n = part(b)
                    pool.wait_ge(peaked, b + 1)
                    pool.tensor_tensor(s, s, peak[:, b % SCB, :].unsqueeze(2).to_broadcast([P, SW_HEADS, n]),
                                       ALU.subtract).then_inc(shifted, 1)

                shift(0)
                shift(1)
                for b in range(NB):
                    s, n = part(b)
                    pool.wait_ge(summed, b + 1)
                    if b:
                        pool.wait_ge(pt_done, 2 * b)
                        pool.wait_ge(probs_done, b)
                    else:
                        pool.wait_ge(pool_sw, 1)
                    pool.tensor_tensor(prob[:, :, 256 - n:], s, total[:, b % SCB, :].unsqueeze(2).to_broadcast([P, SW_HEADS, n]),
                                       ALU.mult).then_inc(probs_done, 1)
                    if b + 2 < NB:
                        shift(b + 2)

            @block.tensor
            def _(pe):
                pe.wait_ge(in_wsw, 16)
                for j in range(4):
                    for i in range(2):
                        for k in range(KT):
                            m = pe.matmul(pb[:, 2 * j + i, :], wsw[:, j, k, :], hT[:, k, i * HALF:(i + 1) * HALF],
                                          start=(k == 0), stop=(k == KT - 1))
                        m.then_inc(sw_proj_done, 1)
                for i in range(2):
                    pe.wait_ge(sw_act if i == 0 else sw_dve, 1)
                    for k in range(KT):
                        m = pe.matmul(pb[:, i, :], wsw[:, 4, k, :], hT[:, k, i * HALF:(i + 1) * HALF],
                                      start=(k == 0), stop=(k == KT - 1))
                    m.then_inc(sw_proj_done, 1)
                for b in range(NB):
                    if b % 4 == 0:
                        pe.wait_ge(sw_act if b == 0 else sw_dve, 2)
                    for k in range(KT):
                        m = pe.matmul(pb[:, 2 + b // 4, (b % 4) * P:(b % 4 + 1) * P], hT[:, k, b * P:(b + 1) * P],
                                      wsw[:, 5, k, :], start=(k == 0), stop=(k == KT - 1))
                    if b % 4 == 3:
                        m.then_inc(sw_proj_done, 1)
                pe.wait_ge(sw_act, 6)
                pe.wait_ge(sw_dve, 6)

                def scores(b):
                    off = CHUNK if b == 0 else 0
                    if b:
                        pe.wait_ge(biased, b)
                    for g in range(2):
                        for j in range(4):
                            a = (j % 2) * BAND
                            m = pe.matmul(pb[:, 2 * g + j // 2, a + off:a + BAND], qb[64 * g:64 * g + 64, j, b * P:(b + 1) * P],
                                          kb[64 * g:64 * g + 64, b * P - CHUNK + off:(b + 1) * P], start=True, stop=True)
                    m.then_inc(sc_done, 1)

                scores(0)
                scores(1)
                for b in range(NB):
                    if b + 2 < NB:
                        scores(b + 2)
                    pe.wait_ge(probs_done, b + 1)
                    for r in range(2):
                        if b:
                            pe.wait_ge(pt_act, 4 * b - 2 + 2 * r)
                            pe.wait_ge(ysw_taken, b)
                        for h in range(4 * r, 4 * r + 4):
                            for w in range(1 if b == 0 else 0, 2):
                                q = (h % 4) * 2 + w
                                m = pe.transpose(pb[:, 4 + 2 * r + q // 4, (q % 4) * P:(q % 4 + 1) * P],
                                                 prob[:, h, w * P:(w + 1) * P], ident[:])
                        m.then_inc(pt_done, 1)
                    pe.wait_ge(pt_act, 4 * b + 4)
                    for h in range(SW_HEADS):
                        g, j = h // 4, h % 4
                        for w in range(1 if b == 0 else 0, 2):
                            m = pe.matmul(pb[64 * g:64 * g + 64, 4, j * P:(j + 1) * P], vb[:, b - 1 + w, 64 * g:64 * g + 64],
                                          pT[:, h, w, :], start=(w == 0 or b == 0), stop=(w == 1))
                    m.then_inc(ysw_done, 1)

            @block.scalar
            def _(act):
                for j in range(4):
                    act.wait_ge(sw_proj_done, 2 * j + 1)
                    act.activation(qb[:, j, 0:HALF], pb[:, 2 * j, :], ACT.Copy).then_inc(sw_act, 1)
                act.wait_ge(sw_proj_done, 9)
                act.activation(kb[:, 0:HALF], pb[:, 0, :], ACT.Copy).then_inc(sw_act, 1)
                act.wait_ge(sw_proj_done, 11)
                act.activation(vb[:, 0:4, :].rearrange("p a b -> p (a b)"), pb[:, 2, :], ACT.Copy).then_inc(sw_act, 1)

                def exponentials(b):
                    act.wait_ge(shifted, b + 1)
                    act.activation(sink_e[:, b % SCB, :], sink_e[:, b % SCB, :], ACT.Exp)
                    s = sc2[:, b % SCB, :].rearrange("p (h n) -> p h n", h=SW_HEADS)[:, :, (CHUNK if b == 0 else 0):]
                    act.activation(s, s, ACT.Exp).then_inc(exp_done, 1)

                exponentials(0)
                exponentials(1)
                for b in range(NB):
                    w0 = 1 if b == 0 else 0
                    if b:
                        act.wait_ge(ysw_done, b)
                    for i in range(4):
                        act.wait_ge(pt_done, 2 * b + 1 + i // 2)
                        act.activation(pT[:, 2 * i:2 * i + 2, w0:, :], pb[:, 4 + i, :].rearrange("p (h w t) -> p h w t", h=2, w=2)[:, :, w0:, :],
                                       ACT.Copy).then_inc(pt_act, 1)
                    act.wait_ge(ysw_done, b + 1)
                    act.activation(yswT[:, :, b * P:(b + 1) * P], pb[:, 4, :].rearrange("p (j t) -> p j t", j=4),
                                   ACT.Copy).then_inc(ysw_taken, 1)
                    if b + 2 < NB:
                        exponentials(b + 2)

            @block.vector
            def _(dve):
                link = Chain(dve, dve_sw)
                for j in range(4):
                    dve.wait_ge(sw_proj_done, 2 * j + 2)
                    dve.tensor_copy(qb[:, j, HALF:S], pb[:, 2 * j + 1, :]).then_inc(sw_dve, 1)
                dve.wait_ge(sw_proj_done, 10)
                dve.tensor_copy(kb[:, HALF:S], pb[:, 1, :]).then_inc(sw_dve, 1)
                dve.wait_ge(sw_proj_done, 12)
                dve.tensor_copy(vb[:, 4:8, :].rearrange("p a b -> p (a b)"), pb[:, 3, :]).then_inc(sw_dve, 1)

                def top(b):
                    s, n = part(b)
                    dve.wait_ge(sc_done, b + 1)
                    if b >= SCB:
                        dve.wait_ge(probs_done, b - SCB + 1)
                    if b == 0:
                        for q in range(4):
                            k = slice(2 * q, 2 * q + 2)
                            t = big[:, 0:TABLE].rearrange("p (h n) -> p h n", h=SW_HEADS)
                            op = dve.scalar_tensor_tensor(out=s[:, k, :], in0=pb[:, q, 0:2 * BAND].rearrange("p (h n) -> p h n", h=2)[:, :, CHUNK:],
                                                          scalar=SCALE, in1=t[:, k, CHUNK:], op0=ALU.mult, op1=ALU.add)
                    else:
                        op = dve.scalar_tensor_tensor(out=sc2[:, b % SCB, :].rearrange("p (q n) -> p q n", q=4), in0=pb[:, 0:4, 0:2 * BAND],
                                                      scalar=SCALE, in1=big[:, 0:TABLE].rearrange("p (q n) -> p q n", q=4),
                                                      op0=ALU.mult, op1=ALU.add)
                    op.then_inc(biased, 1)
                    dve.wait_ge(biased, b + 1)
                    link(dve.tensor_reduce(peak[:, b % SCB, :], s, AX, ALU.max))
                    link(dve.tensor_tensor(peak[:, b % SCB, :], peak[:, b % SCB, :], sink_row[:], ALU.max))
                    dve.tensor_tensor(sink_e[:, b % SCB, :], sink_row[:], peak[:, b % SCB, :], ALU.subtract).then_inc(peaked, 1)

                top(0)
                top(1)
                for b in range(NB):
                    s, n = part(b)
                    dve.wait_ge(exp_done, b + 1)
                    link(dve.tensor_reduce(total[:, b % SCB, :], s, AX, ALU.add))
                    link(dve.tensor_tensor(total[:, b % SCB, :], total[:, b % SCB, :], sink_e[:, b % SCB, :], ALU.add))
                    dve.reciprocal(total[:, b % SCB, :], total[:, b % SCB, :]).then_inc(summed, 1)
                    if b + 2 < NB:
                        top(b + 2)

        gate_mm = sem("gate_mm")
        gate_sig = sem("gate_sig")
        branch_mm = sem("branch_mm")
        gated = sem("gated")
        merged_done = sem("merged_done")
        in_wout = sem("in_wout")
        in_wmg2 = [sem("in_wmg0"), sem("in_wmg1")]
        wmg = at(R4, 6144).rearrange("p (u k f) -> p u k f", u=2, k=24)
        sig = rows(R4 + 6144, 4, HALF)
        mergedT = rows(R2, KT, S)
        wout = rows(R1, KT, D)

        with nc.Block() as block:
            @block.sync
            def _(sp):
                for u in range(2):
                    sp.dma_start(at(R4 + 3072 * u, 3072), w_mg[u]).then_inc(in_wmg2[u], 16)
                sp.dma_start(at(R1, 8192), w_out).then_inc(in_wout, 16)
                with sp.Fori(0, KT // 2 - 1) as t:
                    for u in range(2):
                        sp.wait_ge(branch_mm, t * 8 + 4 * u + 4)
                        sp.dma_start(at(R4 + 3072 * u, 3072), w_mg[bass.ds(t * 2 + 2 + u, 1)].rearrange("a p f -> (a p) f")).then_inc(in_wmg2[u], 16)

            @block.tensor
            def _(pe):
                with pe.Fori(0, KT // 2) as t:
                    for u in range(2):
                        pe.wait_ge(in_wmg2[u], t * 16 + 16)
                        for q in range(4):
                            pe.wait_ge(gate_sig, LED + t * 8 + 4 * u)
                            for k in range(KT):
                                m = pe.matmul(pb[:, q, :], wmg[:, u, (q // 2) * KT + k, :], hT[:, k, (q % 2) * HALF:(q % 2 + 1) * HALF],
                                              start=(k == 0), stop=(k == KT - 1))
                            m.then_inc(gate_mm, 1)
                        pe.wait_ge(gated, LED + t * 8 + 4 * u)
                        for q in range(4):
                            y = ysbT if q < 2 else yswT
                            for k in range(4):
                                m = pe.matmul(pb[:, 4 + q, :], wmg[:, u, 16 + (q // 2) * 4 + k, :], y[:, k, (q % 2) * HALF:(q % 2 + 1) * HALF],
                                              start=(k == 0), stop=(k == 3))
                            m.then_inc(branch_mm, 1)

            @block.scalar
            def _(act):
                lead(act, gate_sig)
                with act.Fori(0, KT // 2) as t:
                    for u in range(2):
                        act.wait_ge(merged_done, LED + t * 4 + 2 * u)
                        for q in range(4):
                            act.wait_ge(gate_mm, t * 8 + 4 * u + q + 1)
                            act.activation(sig[:, q, :], pb[:, q, :], ACT.Sigmoid).then_inc(gate_sig, 1)

            @block.vector
            def _(dve):
                lead(dve, gated, merged_done)
                with dve.Fori(0, KT // 2) as t:
                    for u in range(2):
                        for q in range(4):
                            dve.wait_ge(gate_sig, LED + t * 8 + 4 * u + q + 1)
                            dve.wait_ge(branch_mm, t * 8 + 4 * u + q + 1)
                            dve.tensor_tensor(sig[:, q, :], sig[:, q, :], pb[:, 4 + q, :], ALU.mult).then_inc(gated, 1)
                        dve.wait_ge(gated, LED + t * 8 + 4 * u + 4)
                        for i in range(2):
                            dve.tensor_tensor(mergedT[:, bass.ds(t * 2 + u, 1), i * HALF:(i + 1) * HALF].rearrange("p a b -> p (a b)"),
                                              sig[:, i, :], sig[:, 2 + i, :], ALU.add).then_inc(merged_done, 1)

        out_mm = sem("out_mm")
        x1_scaled = sem("x1_scaled")
        x1_done = sem("x1_done")
        x1_square = sem("x1_square")
        in_x2 = [sem(f"in_x2_{b}") for b in range(NB)]
        rinv2 = sem("rinv2")
        rstd2 = sem("rstd2")
        h2_done = sem("h2_done")
        tr2_done = sem("tr2_done")
        tr2_act = sem("tr2_act")
        tr2_dve = sem("tr2_dve")
        dve_o = sem("dve_o")
        x1_stored = sem("x1_stored")
        h2 = rows(R4, NB, D)
        h2T = hT

        with nc.Block() as block:
            @block.sync
            def _(sp):
                for b in range(NB):
                    sp.dma_start(xt[:, b, :], x[b * P:(b + 1) * P, :]).then_inc(in_x2[b], 16)
                for b in range(NB):
                    sp.wait_ge(x1_done, b + 1)
                    sp.dma_start(x1_dram[b * P:(b + 1) * P, :], xt[:, b, :]).then_inc(x1_stored, 16)

            @block.tensor
            def _(pe):
                def transposes(b):
                    pe.wait_ge(h2_done, b + 1)
                    if b >= 2:
                        pe.wait_ge(tr2_act, b - 1)
                        pe.wait_ge(tr2_dve, b - 1)
                    for k in range(KT):
                        t = pe.transpose(pb[:, 4 + 2 * (b % 2) + k // 4, (k % 4) * P:(k % 4 + 1) * P],
                                         h2[:, b, k * P:(k + 1) * P], ident[:])
                        if k % 4 == 3:
                            t.then_inc(tr2_done, 1)

                pe.wait_ge(in_wout, 16)
                for b in range(NB):
                    if b >= 2:
                        pe.wait_ge(x1_scaled, b - 1)
                    for i in range(2):
                        for k in range(KT):
                            m = pe.matmul(pb[:, 2 * (b % 2) + i, :], mergedT[:, k, b * P:(b + 1) * P], wout[:, k, i * HALF:(i + 1) * HALF],
                                          start=(k == 0), stop=(k == KT - 1))
                    m.then_inc(out_mm, 1)
                    if b:
                        transposes(b - 1)
                transposes(NB - 1)

            @block.scalar
            def _(act):
                for b in range(NB):
                    act.wait_ge(x1_done, b + 1)
                    act.activation(h2[:, b, :], xt[:, b, :], ACT.Square, accum_out=stats[:, b:b + 1]).then_inc(x1_square, 1)
                    act.wait_ge(rinv2, b + 1)
                    act.activation(stats[:, 16 + b:17 + b], stats[:, 8 + b:9 + b], ACT.Sqrt).then_inc(rstd2, 1)
                    if b:
                        act.wait_ge(tr2_done, 2 * b - 1)
                        act.activation(h2T[:, 0:4, (b - 1) * P:b * P], pb[:, 4 + 2 * ((b - 1) % 2), :].rearrange("p (a b) -> p a b", a=4),
                                       ACT.Copy).then_inc(tr2_act, 1)
                act.wait_ge(tr2_done, 2 * NB - 1)
                act.activation(h2T[:, 0:4, S - P:S], pb[:, 4 + 2 * ((NB - 1) % 2), :].rearrange("p (a b) -> p a b", a=4),
                               ACT.Copy).then_inc(tr2_act, 1)

            @block.vector
            def _(dve):
                link = Chain(dve, dve_o)

                def residual(b):
                    dve.wait_ge(out_mm, b + 1)
                    dve.tensor_tensor(h2[:, b, :], pb[:, 2 * (b % 2):2 * (b % 2) + 2, :].rearrange("p a b -> p (a b)"), mod(GATE1),
                                      ALU.mult).then_inc(x1_scaled, 1)
                    dve.wait_ge(x1_scaled, b + 1)
                    dve.wait_ge(in_x2[b], 16)
                    dve.tensor_tensor(xt[:, b, :], xt[:, b, :], h2[:, b, :], ALU.add).then_inc(x1_done, 1)

                def take(b):
                    dve.wait_ge(tr2_done, 2 * b + 2)
                    dve.tensor_copy(h2T[:, 4:8, b * P:(b + 1) * P],
                                    pb[:, 5 + 2 * (b % 2), :].rearrange("p (a b) -> p a b", a=4)).then_inc(tr2_dve, 1)

                for b in range(NB):
                    residual(b)
                    dve.wait_ge(x1_square, b + 1)
                    link(dve.tensor_scalar(stats[:, 24 + b:25 + b], stats[:, b:b + 1], 1.0 / D, EPS, ALU.mult, ALU.add))
                    dve.reciprocal(stats[:, 8 + b:9 + b], stats[:, 24 + b:25 + b]).then_inc(rinv2, 1)
                    if b:
                        take(b - 1)
                    dve.wait_ge(rstd2, b + 1)
                    link(dve.scalar_tensor_tensor(out=h2[:, b, :], in0=xt[:, b, :], scalar=stats[:, 16 + b:17 + b],
                                                  in1=mod(SCALE2), op0=ALU.mult, op1=ALU.mult))
                    dve.tensor_tensor(h2[:, b, :], h2[:, b, :], mod(SHIFT2), ALU.add).then_inc(h2_done, 1)
                take(NB - 1)

        gathered = [sem(f"gathered{i}") for i in range(RING)]
        ring_free = sem("ring_free")
        acc_free = sem("acc_free")
        zeroed = sem("zeroed")
        in_wqn = sem("in_wqn")
        q_mm = sem("q_mm")
        q_taken = sem("q_taken")
        s_mm = sem("s_mm")
        s_taken = sem("s_taken")
        s_used = sem("s_used")
        picked = sem("picked")
        picked_exp = sem("picked_exp")
        published = sem("published")
        dots_done = sem("dots_done")
        gelu_done = sem("gelu_done")
        diag_done = sem("diag_done")
        idg_done = sem("idg_done")
        dve_p = sem("dve_p")
        ring = rows(R3, RING, 2 * D)
        acc = rows(R2, NB, D)
        wq = at(MODS, 2048).rearrange("p (a k f) -> p a k f", a=2, k=KT)
        qpT = at(MODS + 2 * D, S)
        ssb = rows(MODS + 3 * D, NB, NKEYS)
        tiny = MODS + 4 * D
        vals = [rows(tiny + 128 * i, NB, TOPK) for i in range(2)]
        best = rows(tiny + 256, NB, TOPK)
        fl = [rows(tiny + 384 + 128 * i, NB, TOPK) for i in range(2)]
        res = [rows(tiny + 640 + 128 * i, NB, TOPK) for i in range(2)]
        gate_next = rows(tiny + 896, NB, TOPK)
        kidx = [sb(f"kidx{i}", [P, NB, TOPK], U32) for i in range(2)]
        bidx = sb("bidx", [P, NB, TOPK], U32)
        part_u = sb("part_u", [P, NB, TOPK], U32)
        idx_next = sb("idx_next", [P, PICKS], U32)
        idx_cur = sb("idx_cur", [P, PICKS], U32)
        gate_cur = sb("gate_cur", [P, PICKS])
        sks = sb("sks", [P, 2, NKEYS])
        dots = sb("dots", [P, RING])
        gl = sb("gl", [P, 4])
        idg = sb("idg", [P, 4, P])
        dg = sb("dg", [P, 4, P])
        norm = sb("norm", [P, NB])
        cand = big[:].rearrange("p (b i j) -> p b i j", b=NB, i=TOPK)
        SPLITS = (0, PICKS // 2, 96)
        OWN = NB // 2
        DVE_PER_TURN = 2 * NB * 4 + 1 + NB * 4 + 1 + 12 + 6 + 2

        Q_AT = (0, 20)
        S_AT = (18, 38)
        TOP_AT = (22, 44)
        CAND_AT, BEST_AT, DECODE_AT = 53, 54, 74

        with nc.Block() as block:
            @block.sync
            def _(sp):
                sp.dma_start(sks[:].rearrange("p a n -> p (a n)"), sk[0]).then_inc(in_wqn, 16)
                sp.wait_ge(x1_stored, 16 * NB)
                with sp.Fori(0, HEADS - 1) as t:
                    sp.wait_ge(s_mm, t * 2 + 2)
                    sp.dma_start(at(MODS, 2048), w_q[bass.ds(t + 1, 1)].rearrange("a p f -> (a p) f")).then_inc(in_wq, 16)
                    sp.dma_start(sks[:].rearrange("p a n -> p (a n)"), sk[bass.ds(t + 1, 1)].rearrange("a p f -> (a p) f")).then_inc(in_wqn, 16)

            @block.gpsimd
            def _(pool):
                pool.memset(at(R2, 8192), 0.0).then_inc(zeroed, 1)
                pool.wait_ge(x1_stored, 16 * NB)

                def gathers(t):
                    for n in range(PICKS):
                        if n in SPLITS:
                            pool.wait_ge(published, t * 3 + SPLITS.index(n) + 1)
                        pool.wait_ge(ring_free, t * PICKS + n + 1)
                        apart(pool, pool_steps)
                        pool.indirect_dma_start(ring[:, n % RING, :], None, uv,
                                                bass.IndirectOffsetOnAxis(ap=idx_cur[:, n:n + 1], axis=0)).then_inc(gathered[n % RING], 16)

                with pool.Fori(0, HEADS) as t:
                    gathers(t)

            @block.tensor
            def _(pe):
                def project(h, p, i):
                    half, k = i // KT, i % KT
                    if p == 0 and i == 0:
                        pe.wait_ge(in_wq, h * 16 + 16)
                        pe.wait_ge(in_wqn, h * 16 + 16)
                    if i == 0:
                        pe.wait_ge(q_taken, h * 4 + 2 * p)
                    m = pe.matmul(pb[:, half, :], wq[:, p, k, :], h2T[:, k, half * HALF:(half + 1) * HALF],
                                  start=(k == 0), stop=(k == KT - 1))
                    if k == KT - 1:
                        m.then_inc(q_mm, 1)

                def half_scores(h, p, b):
                    if b == 0:
                        pe.wait_ge(q_taken, h * 4 + 2 * p + 2)
                        pe.wait_ge(s_taken, h * 4 + 2 * p)
                    m = pe.matmul(pb[:, 2 + b // 4, (b % 4) * P:(b % 4 + 1) * P], qpT[:, b * P:(b + 1) * P], sks[:, p, :],
                                  start=True, stop=True)
                    if b == NB - 1:
                        m.then_inc(s_mm, 1)

                def turn(t, keys):
                    for n in range(PICKS):
                        if keys:
                            for p in range(2):
                                if Q_AT[p] <= n < Q_AT[p] + 16:
                                    project(t + 1, p, n - Q_AT[p])
                                if S_AT[p] <= n < S_AT[p] + 2:
                                    for b in range(4 * (n - S_AT[p]), 4 * (n - S_AT[p]) + 4):
                                        half_scores(t + 1, p, b)
                        b, k = n // TOPK, n % TOPK
                        if k == 0:
                            pe.wait_ge(acc_free, t * NB + b + 1)
                        pe.wait_ge(diag_done, LED + t * PICKS + n + 1)
                        for i in range(2):
                            m = pe.matmul(pb[:, 4 + 2 * (b % 2) + i, :], dg[:, n % 4, :],
                                          ring[:, n % RING, D + i * HALF:D + (i + 1) * HALF], start=(k == 0), stop=(k == TOPK - 1))
                        m.then_inc(ring_free, 1)

                pe.sem_inc(ring_free, RING)
                pe.sem_inc(acc_free, 2)
                pe.wait_ge(in_wq, 16)
                pe.wait_ge(in_wqn, 16)
                for i in range(2):
                    for p in range(2):
                        if i:
                            pe.wait_ge(q_taken, p + 1)
                        for k in range(KT):
                            m = pe.matmul(pb[:, p, :], wq[:, p, k, :], h2T[:, k, i * HALF:(i + 1) * HALF],
                                          start=(k == 0), stop=(k == KT - 1))
                        m.then_inc(q_mm, 1)
                    pe.wait_ge(q_taken, 2 * i + 2)
                    if i:
                        pe.wait_ge(s_taken, 2)
                    for p in range(2):
                        for b in range(OWN):
                            m = pe.matmul(pb[:, 2 + p, b * P:(b + 1) * P], qpT[:, p * HALF + b * P:p * HALF + (b + 1) * P],
                                          sks[:, p, :], start=True, stop=True)
                    m.then_inc(s_mm, 1)
                with pe.Fori(0, HEADS - 1) as t:
                    turn(t, True)
                turn(HEADS - 1, False)

            @block.scalar
            def _(act):
                def take_query(h, p, i):
                    act.wait_ge(q_mm, h * 4 + 2 * p + i + 1)
                    act.wait_ge(s_mm, h * 2 + p)
                    act.activation(qpT[:, i * HALF:(i + 1) * HALF], pb[:, i, :], ACT.Copy).then_inc(q_taken, 1)

                def take_scores(h, p):
                    act.wait_ge(s_mm, h * 2 + p + 1)
                    act.wait_ge(s_used, h * 2 + p)
                    for i in range(2):
                        act.activation(ssb[:, 4 * i:4 * i + 4, :].rearrange("p a b -> p (a b)"), pb[:, 2 + i, :], ACT.Copy).then_inc(s_taken, 1)

                def gate_exp(count, blocks=slice(0, NB)):
                    act.wait_ge(picked, count)
                    act.activation(best[:, blocks], best[:, blocks], ACT.Exp).then_inc(picked_exp, 1)

                def scaled_identity(t, n):
                    if n in SPLITS:
                        act.wait_ge(published, t * 3 + SPLITS.index(n) + 1)
                    act.wait_ge(diag_done, LED + t * PICKS + max(n - 3, 0))
                    act.activation(idg[:, n % 4, :], ident[:], ACT.Copy, scale=gate_cur[:, n:n + 1]).then_inc(idg_done, 1)

                def turn(t, keys):
                    for n in (0, 1):
                        scaled_identity(t, n)
                    for n in range(0, PICKS, 2):
                        for m in (n + 2, n + 3):
                            if m < PICKS:
                                scaled_identity(t, m)
                        act.wait_ge(dots_done, t * PICKS + n + 2)
                        act.wait_ge(diag_done, LED + t * PICKS + n)
                        act.activation(gl[:, 0:2], dots[:, n % RING:n % RING + 2], ACT.Gelu).then_inc(gelu_done, 1)
                        act.wait_ge(gelu_done, t * (PICKS // 2) + n // 2 + 1)
                        act.wait_ge(idg_done, t * PICKS + n + 2)
                        for m in (n, n + 1):
                            act.wait_ge(ring_free, t * PICKS + m - 3 + RING)
                            act.activation(dg[:, m % 4, :], idg[:, m % 4, :], ACT.Copy, scale=gl[:, m - n:m - n + 1]).then_inc(diag_done, 1)
                        if keys:
                            for p in range(2):
                                if n in (Q_AT[p] + 10, Q_AT[p] + 18 - 2):
                                    take_query(t + 1, p, 0 if n == Q_AT[p] + 10 else 1)
                                if n == S_AT[p] + 2:
                                    take_scores(t + 1, p)
                            if n == DECODE_AT + 16:
                                gate_exp(t + 3)

                lead(act, diag_done)
                for i in range(2):
                    for p in range(2):
                        act.wait_ge(q_mm, 2 * i + p + 1)
                        if i:
                            act.wait_ge(s_mm, 1)
                        act.activation(qpT[:, p * HALF:(p + 1) * HALF], pb[:, p, :], ACT.Copy).then_inc(q_taken, 1)
                    act.wait_ge(s_mm, i + 1)
                    if i:
                        act.wait_ge(s_used, 1)
                    for p in range(2):
                        act.activation(ssb[:, OWN * p:OWN * (p + 1), :].rearrange("p a b -> p (a b)"), pb[:, 2 + p, :],
                                       ACT.Copy).then_inc(s_taken, 1)
                for i in range(2):
                    gate_exp(i + 1, slice(OWN * i, OWN * (i + 1)))
                with act.Fori(0, HEADS - 1) as t:
                    turn(t, True)
                turn(HEADS - 1, False)

            @block.vector
            def _(dve):
                link = Chain(dve, dve_p)

                def top16(values, indices, scores):
                    apart(dve, dve_steps)
                    link(dve.max(values[:, 0:8], scores))
                    apart(dve, dve_steps)
                    link(dve.max_index(indices[:, 0:8], values[:, 0:8], scores))
                    apart(dve, dve_steps)
                    link(dve.match_replace(scores, values[:, 0:8], scores, LOWEST))
                    apart(dve, dve_steps)
                    link(dve.max(values[:, 8:16], scores))
                    apart(dve, dve_steps)
                    return dve.max_index(indices[:, 8:16], values[:, 8:16], scores)

                def top_half(h, p, b):
                    if b == 0:
                        dve.wait_ge(s_taken, h * 4 + 2 * p + 2)
                    op = top16(vals[p][:, b, :], kidx[p][:, b, :], ssb[:, b, :])
                    if b == NB - 1:
                        op.then_inc(s_used, 1)

                def candidates(used, blocks=slice(0, NB)):
                    dve.wait_ge(s_used, used)
                    n = blocks.stop - blocks.start
                    link(dve.tensor_tensor(cand[:, blocks], vals[0][:, blocks].unsqueeze(3).to_broadcast([P, n, TOPK, TOPK]),
                                           vals[1][:, blocks].unsqueeze(2).to_broadcast([P, n, TOPK, TOPK]), ALU.add))

                def top_pairs(b, last=NB - 1):
                    op = top16(best[:, b, :], bidx[:, b, :], cand[:, b].rearrange("p i j -> p (i j)"))
                    if b == last:
                        link(op)

                def decode(count, step, blocks=slice(0, NB)):
                    p = 0 if step < 6 else 1
                    n = blocks.stop - blocks.start
                    picks = slice(blocks.start * TOPK, blocks.stop * TOPK)
                    wide = cand.rearrange("p b k i -> p (b k) i")[:, picks]
                    f = fl[p].rearrange("p b k -> p (b k)")[:, picks]
                    first, second = (r.rearrange("p b k -> p (b k)")[:, picks] for r in res)
                    part = part_u[:, blocks]
                    top = best[:, blocks]
                    q = step % 6
                    if step < 12 and q == 0:
                        if p == 0:
                            link(dve.tensor_scalar(part, bidx[:, blocks], 4, None, ALU.logical_shift_right))
                        else:
                            link(dve.tensor_scalar(part, bidx[:, blocks], TOPK - 1, None, ALU.bitwise_and))
                    elif step < 12 and q == 1:
                        link(dve.tensor_copy(f, part_u[:].rearrange("p b k -> p (b k)")[:, picks]))
                    elif step < 12 and q == 2:
                        link(dve.tensor_tensor(wide, f.unsqueeze(2).to_broadcast([P, n * TOPK, TOPK]),
                                               iota16[:].unsqueeze(1).to_broadcast([P, n * TOPK, TOPK]), ALU.is_equal))
                    elif step < 12 and q == 3:
                        link(dve.tensor_copy(fl[p][:, blocks], kidx[p][:, blocks]))
                    elif step < 12 and q == 4:
                        link(dve.tensor_tensor(cand[:, blocks], cand[:, blocks],
                                               fl[p][:, blocks].unsqueeze(2).to_broadcast([P, n, TOPK, TOPK]), ALU.mult))
                    elif step < 12:
                        link(dve.tensor_reduce(second if p else first, wide, AX, ALU.add))
                    elif step == 12:
                        link(dve.scalar_tensor_tensor(out=first, in0=first, scalar=float(NKEYS), in1=second, op0=ALU.mult, op1=ALU.add))
                        link(dve.tensor_copy(idx_next[:, picks], first))
                        link(dve.tensor_copy(norm[:, blocks], best[:, blocks, 0]))
                        dve.tensor_tensor(top, top, norm[:, blocks].unsqueeze(2).to_broadcast([P, n, TOPK]), ALU.subtract).then_inc(picked, 1)
                    else:
                        dve.wait_ge(picked_exp, count)
                        link(dve.tensor_reduce(norm[:, blocks], top, AX, ALU.add))
                        link(dve.reciprocal(norm[:, blocks], norm[:, blocks]))
                        link(dve.tensor_tensor(gate_next[:, blocks], top, norm[:, blocks].unsqueeze(2).to_broadcast([P, n, TOPK]), ALU.mult))

                def publish(a, b, parts, before=None):
                    if before is not None:
                        dve.wait_ge(diag_done, LED + before)
                    link(dve.tensor_copy(idx_cur[:, a:b], idx_next[:, a:b]))
                    dve.tensor_copy(gate_cur[:, a:b], gate_next.rearrange("p b k -> p (b k)")[:, a:b]).then_inc(published, parts)

                def add_block(t, b, last):
                    dve.wait_ge(ring_free, t * PICKS + b * TOPK + TOPK + RING)
                    dve.wait_ge(acc_free, t * NB + b + 2)
                    dve.tensor_tensor(acc[:, b, :], acc[:, b, :], pb[:, 4 + 2 * (b % 2):6 + 2 * (b % 2), :].rearrange("p a b -> p (a b)"),
                                      ALU.add).then_inc(acc_free, 1)
                    if last:
                        dve.wait_ge(acc_free, t * NB + b + 3)
                        dve.tensor_tensor(acc[:, b, :], acc[:, b, :], mod(GATE2), ALU.mult)

                def turn(t, keys):
                    for n in range(PICKS):
                        b = n // TOPK
                        dve.wait_ge(gathered[n % RING], t * (PICKS // RING * 16) + 16 * (n // RING) + 16)
                        u = ring[:, n % RING, 0:D]
                        dve.tensor_tensor_reduce(u, h2[:, b, :], u, 1.0, 0.0, ALU.mult, ALU.add,
                                                 dots[:, n % RING:n % RING + 1]).then_inc(dots_done, 1)
                        if b and n % TOPK == 4:
                            add_block(t, b - 1, not keys)
                        if keys:
                            for p in range(2):
                                if TOP_AT[p] <= n < TOP_AT[p] + NB:
                                    top_half(t + 1, p, n - TOP_AT[p])
                            if n == CAND_AT:
                                candidates(t * 2 + 4)
                            if BEST_AT <= n < BEST_AT + 2 * NB and (n - BEST_AT) % 2 == 0:
                                top_pairs((n - BEST_AT) // 2)
                            if DECODE_AT <= n < DECODE_AT + 13:
                                decode(None, n - DECODE_AT)
                            if n == DECODE_AT + 22:
                                decode(t + 3, 13)
                            if n == PICKS - 12:
                                publish(0, SPLITS[2], 2, t * PICKS + SPLITS[2])
                    if keys:
                        publish(SPLITS[2], PICKS, 1, t * PICKS + PICKS)
                    add_block(t, NB - 1, not keys)

                dve.wait_ge(zeroed, 1)
                for i in range(2):
                    blocks = slice(OWN * i, OWN * (i + 1))
                    dve.wait_ge(s_taken, 2 * i + 2)
                    for p in range(2):
                        for b in range(OWN):
                            op = top16(vals[p][:, OWN * i + b, :], kidx[p][:, OWN * i + b, :], ssb[:, OWN * p + b, :])
                    op.then_inc(s_used, 1)
                    candidates(i + 1, blocks)
                    for b in range(OWN * i, OWN * (i + 1)):
                        top_pairs(b, blocks.stop - 1)
                    for step in range(14):
                        decode(i + 1, step, blocks)
                    if i == 0:
                        publish(0, SPLITS[1], 1)
                    else:
                        publish(SPLITS[1], PICKS, 2)
                with dve.Fori(0, HEADS - 1) as t:
                    before = link.n
                    link.enter(t, DVE_PER_TURN)
                    turn(t, True)
                    link.leave(HEADS - 1)
                turn(HEADS - 1, False)

        in_x1 = [sem(f"in_x1_{b}") for b in range(NB)]
        in_gf = sem("in_gf")
        f_sum = sem("f_sum")
        f_square = sem("f_square")
        f_rinv = sem("f_rinv")
        f_rstd = sem("f_rstd")
        f_done = sem("f_done")
        f_own = sem("f_own")
        out_stored = sem("out_stored")
        final_g = at(MODS, D)
        xf = rows(R3, NB, D)
        junk = at(MODS + D, D)

        with nc.Block() as block:
            @block.sync
            def _(sp):
                sp.dma_start(final_g, gf.partition_broadcast(P)).then_inc(in_gf, 16)
                for b in range(NB):
                    sp.dma_start(xf[:, b, :], x1_dram[b * P:(b + 1) * P, :]).then_inc(in_x1[b], 16)
                for b in range(NB):
                    sp.wait_ge(f_done, b + 1)
                    sp.dma_start(out[b * P:(b + 1) * P, :], acc[:, b, :]).then_inc(out_stored, 16)
                sp.wait_ge(out_stored, 16 * NB)

            @block.scalar
            def _(act):
                for b in range(NB):
                    act.wait_ge(f_sum, b + 1)
                    act.wait_ge(f_square, b)
                    act.activation(junk, acc[:, b, :], ACT.Square, accum_out=stats[:, b:b + 1]).then_inc(f_square, 1)
                    act.wait_ge(f_rinv, b + 1)
                    act.activation(stats[:, 16 + b:17 + b], stats[:, 8 + b:9 + b], ACT.Sqrt).then_inc(f_rstd, 1)

            @block.vector
            def _(dve):
                link = Chain(dve, f_own)

                def residual(b):
                    dve.wait_ge(in_x1[b], 16)
                    dve.tensor_tensor(acc[:, b, :], acc[:, b, :], xf[:, b, :], ALU.add).then_inc(f_sum, 1)

                dve.wait_ge(in_gf, 16)
                residual(0)
                for b in range(NB):
                    if b + 1 < NB:
                        residual(b + 1)
                    dve.wait_ge(f_square, b + 1)
                    link(dve.tensor_scalar(stats[:, 24 + b:25 + b], stats[:, b:b + 1], 1.0 / D, EPS, ALU.mult, ALU.add))
                    dve.reciprocal(stats[:, 8 + b:9 + b], stats[:, 24 + b:25 + b]).then_inc(f_rinv, 1)
                    dve.wait_ge(f_rstd, b + 1)
                    dve.scalar_tensor_tensor(out=acc[:, b, :], in0=acc[:, b, :], scalar=stats[:, 16 + b:17 + b],
                                             in1=final_g, op0=ALU.mult, op1=ALU.mult).then_inc(f_done, 1)


def shape_constants():
    j, s = np.mgrid[0:P, 0:P]
    tri = -(j >= s).astype(np.float32)
    t, k = np.mgrid[0:P, 0:BAND]
    key = k - CHUNK
    behind = t // CHUNK - key // CHUNK
    seen = (behind == 0) | (behind == 1)
    slopes = 2.0 ** (-8.0 * np.arange(1, SW_HEADS + 1) / SW_HEADS)
    table = np.where(seen[:, None, :], -slopes[None, :, None] * np.abs(t - key)[:, None, :], -1e30)
    iota = np.broadcast_to(np.arange(TOPK, dtype=np.float32), (P, TOPK))
    unseen = np.where(j >= s, -1e30, 0.0)
    return np.concatenate([np.eye(P), tri, iota, table.reshape(P, -1), unseen], axis=1).astype(np.float32)


def kernel(**inputs):
    import concourse.bacc as _bacc
    from concourse.bass_utils import run_bass_kernel_spmd as _run

    a = {k: np.asarray(v) for k, v in inputs.items()}
    w_in = a["w_in"][0]
    sbw = SB_PAIRS * P
    w_sb = w_in[:, :3 * sbw].reshape(KT, P, 3, SB_PAIRS, P).transpose(3, 1, 2, 0, 4).reshape(SB_PAIRS, P, -1)
    o = 3 * sbw
    wq = w_in[:, o:o + 512].reshape(KT, P, 2, 4, DH).transpose(1, 3, 0, 2, 4).reshape(P, 4, KT, P)
    wkv = w_in[:, o + 512:o + 768].reshape(KT, P, 2, P).transpose(1, 2, 0, 3)
    w_sw = np.concatenate([wq, wkv], axis=1).reshape(P, -1)
    gates = w_in[:, o + 768:].reshape(KT, P, 2, KT, P).transpose(3, 1, 2, 0, 4).reshape(KT, P, 2 * KT, P)
    p_sb = a["sb_proj"][0].reshape(4, P, KT, P).transpose(2, 1, 0, 3)
    p_sw = a["sw_proj"][0].reshape(2, 4, DH, D).transpose(1, 0, 2, 3).reshape(4, P, KT, P).transpose(2, 1, 0, 3)
    arrays = {
        "x": a["x"][0],
        "c8": a["c"].reshape(KT, P).T,
        "w_ada": a["w_ada"][0].reshape(KT, P, 12, HALF).transpose(2, 1, 0, 3),
        "b_ada": a["b_ada"],
        "g1": a["norm1_g"][0],
        "g2": a["norm2_g"][0],
        "gf": a["final_g"],
        "w_sb": w_sb,
        "w_sw": w_sw,
        "sinks": a["sw_sinks"][0],
        "w_mg": np.concatenate([gates, p_sb, p_sw], axis=2).reshape(KT, P, -1),
        "w_out": a["w_out"][0].reshape(KT, P, D).transpose(1, 0, 2).reshape(P, -1),
        "w_q": a["peer_wq"][0].reshape(KT, P, HEADS, 2, P).transpose(2, 1, 3, 0, 4).reshape(HEADS, P, -1),
        "sk": a["peer_sub_keys"][0].transpose(0, 3, 1, 2).reshape(HEADS, P, -1),
        "uv": np.concatenate([a["peer_u"][0], a["peer_v"][0]], axis=1),
        "consts": shape_constants(),
    }
    arrays = {k: np.ascontiguousarray(v) for k, v in arrays.items()}
    nc = _bacc.Bacc("TRN2", target_bir_lowering=False, num_devices=1)
    args = [nc.dram_tensor("in_" + k, v.shape, mybir.dt.from_np(v.dtype), kind="ExternalInput").ap() for k, v in arrays.items()]
    args.append(nc.dram_tensor("x1_scratch", (S, D), F32, kind="Internal").ap())
    args.append(nc.dram_tensor("out_0", (S, D), F32, kind="ExternalOutput").ap())
    build(nc, *args)
    r = _run(nc, [{"in_" + k: v for k, v in arrays.items()}], core_ids=[0])
    return r.results[0]["out_0"].reshape(1, S, D)
```
